# Optimizing a Trainium2 kernel written in Bass

```python
import math
import jax, jax.numpy as jnp
from jax import lax
import numpy as np

D_MODEL = 1024
BATCH = 1
SEQ = 512
DEPTH = 1

HEAD_DIM = 64
A_Q_HEADS = 8
A_KV_HEADS = 2
A_GROUP = A_Q_HEADS // A_KV_HEADS
B_HEADS = 4
B_V_DIM = 2 * HEAD_DIM
A_WIDTH = A_Q_HEADS * HEAD_DIM
B_WIDTH = B_HEADS * B_V_DIM
GRID_W = 64
ROPE_THETA = 10000.0
Q_BLOCK = 128
EPS = 1e-6
LN_EPS = 1e-5
PEER_HEADS = 8
PEER_N_KEYS = 128
PEER_N_EXPERTS = PEER_N_KEYS * PEER_N_KEYS
PEER_QUERY_DIM = 256
PEER_HALF = PEER_QUERY_DIM // 2
PEER_TOPK = 16
PEER_TOKEN_BLOCK = 128
DN_ALPHA = (2.0 * DEPTH) ** 0.25
DN_BETA = (8.0 * DEPTH) ** -0.25

COLS_A_Q = A_Q_HEADS * HEAD_DIM
COLS_A_KV = A_KV_HEADS * HEAD_DIM
COLS_B_QK = B_HEADS * 2 * HEAD_DIM
COLS_B_V = B_HEADS * B_V_DIM
COLS_GATES = 2 * D_MODEL
IN_COLS = COLS_A_Q + 2 * COLS_A_KV + 2 * COLS_B_QK + COLS_B_V + COLS_GATES
SPLIT_1 = COLS_A_Q
SPLIT_2 = SPLIT_1 + COLS_A_KV
SPLIT_3 = SPLIT_2 + COLS_A_KV
SPLIT_4 = SPLIT_3 + COLS_B_QK
SPLIT_5 = SPLIT_4 + COLS_B_QK
SPLIT_6 = SPLIT_5 + COLS_B_V

kernel_name = 'hybrid_gqa_diffattn_peer_deepnorm'

def rms_norm(x, g):
    xf = x.astype(jnp.float32)
    y = xf * lax.rsqrt(jnp.mean(xf * xf, axis=-1, keepdims=True) + EPS)
    return (y * g.astype(jnp.float32)).astype(x.dtype)

def layer_norm(x, g, b):
    xf = x.astype(jnp.float32)
    mu = jnp.mean(xf, axis=-1, keepdims=True)
    xc = xf - mu
    var = jnp.mean(xc * xc, axis=-1, keepdims=True)
    y = xc * lax.rsqrt(var + LN_EPS) * g.astype(jnp.float32) + b.astype(jnp.float32)
    return y.astype(x.dtype)

def rope_tables(pos, dim):
    freqs = ROPE_THETA ** (-jnp.arange(0, dim, 2, dtype=jnp.float32) / dim)
    ang = pos.astype(jnp.float32)[:, None] * freqs[None, :]
    return jnp.cos(ang), jnp.sin(ang)

def apply_rope(x, cos, sin):
    xf = x.astype(jnp.float32)
    half = x.shape[-1] // 2
    x1, x2 = xf[..., :half], xf[..., half:]
    c = cos[None, :, None, :]
    s = sin[None, :, None, :]
    return jnp.concatenate([x1 * c - x2 * s, x2 * c + x1 * s], axis=-1).astype(x.dtype)

def apply_axial_rope(x, row_tab, col_tab):
    half = x.shape[-1] // 2
    return jnp.concatenate([apply_rope(x[..., :half], *row_tab),
                            apply_rope(x[..., half:], *col_tab)], axis=-1)

def to_query_blocks(q):
    shape = q.shape
    nb = shape[-2] // Q_BLOCK
    qb = q.reshape(shape[:-2] + (nb, Q_BLOCK, shape[-1]))
    return jnp.moveaxis(qb, -3, 0)

def from_query_blocks(ob):
    ob = jnp.moveaxis(ob, 0, -3)
    shape = ob.shape
    return ob.reshape(shape[:-3] + (shape[-3] * shape[-2], shape[-1]))

def gqa_attention(q, k, v):
    B, S, _, d = q.shape
    qg = q.reshape(B, S, A_KV_HEADS, A_GROUP, d).transpose(0, 2, 3, 1, 4)
    kg = k.transpose(0, 2, 1, 3)
    vg = v.transpose(0, 2, 1, 3)
    scale = d ** -0.5

    def block(qb):
        s = jnp.einsum('bgrqd,bgkd->bgrqk', qb, kg).astype(jnp.float32) * scale
        p = jax.nn.softmax(s, axis=-1)
        return jnp.einsum('bgrqk,bgkd->bgrqd', p.astype(vg.dtype), vg)

    o = from_query_blocks(lax.map(block, to_query_blocks(qg)))
    return o.transpose(0, 3, 1, 2, 4).reshape(B, S, A_WIDTH)

def diff_attention(q, k, v, lam, subln_g, lambda_init):
    B, S, _, _, d = q.shape
    qh = q.transpose(0, 2, 3, 1, 4)
    kh = k.transpose(0, 2, 3, 1, 4)
    vh = v.transpose(0, 2, 1, 3)
    scale = d ** -0.5

    def block(qb):
        s = jnp.einsum('bhiqd,bhikd->bhiqk', qb, kh).astype(jnp.float32) * scale
        p = jax.nn.softmax(s, axis=-1)
        a = p[:, :, 0] - lam * p[:, :, 1]
        return jnp.einsum('bhqk,bhkv->bhqv', a.astype(vh.dtype), vh)

    o = from_query_blocks(lax.map(block, to_query_blocks(qh)))
    o = rms_norm(o, subln_g) * (1.0 - lambda_init)
    return o.transpose(0, 2, 1, 3).reshape(B, S, B_WIDTH)

def peer_ffn(h, w_query, sub_keys, u_table, v_table):
    B, S, D = h.shape
    T = B * S
    hf = h.reshape(T, D)
    q = (hf @ w_query).reshape(T, PEER_HEADS, 2, PEER_HALF)
    s = jnp.einsum('thid,hind->thin', q, sub_keys).astype(jnp.float32)
    sv, si = lax.top_k(s, PEER_TOPK)
    cand = (sv[:, :, 0, :, None] + sv[:, :, 1, None, :]).reshape(T, PEER_HEADS, PEER_TOPK * PEER_TOPK)
    cv, ci = lax.top_k(cand, PEER_TOPK)
    i1 = jnp.take_along_axis(si[:, :, 0, :], ci // PEER_TOPK, axis=-1)
    i2 = jnp.take_along_axis(si[:, :, 1, :], ci % PEER_TOPK, axis=-1)
    experts = i1 * PEER_N_KEYS + i2
    gates = jax.nn.softmax(cv, axis=-1)

    nbt = T // PEER_TOKEN_BLOCK
    hb_all = hf.reshape(nbt, PEER_TOKEN_BLOCK, D)
    e_all = experts.reshape(nbt, PEER_TOKEN_BLOCK, PEER_HEADS, PEER_TOPK)
    g_all = gates.reshape(nbt, PEER_TOKEN_BLOCK, PEER_HEADS, PEER_TOPK)

    def block(args):
        hb, eb, gb = args
        u = jnp.take(u_table, eb, axis=0)
        a = jnp.einsum('td,thkd->thk', hb, u).astype(jnp.float32)
        w = jax.nn.gelu(a, approximate=False) * gb
        vv = jnp.take(v_table, eb, axis=0)
        return jnp.einsum('thk,thkd->td', w.astype(hb.dtype), vv)

    y = lax.map(block, (hb_all, e_all, g_all))
    return y.reshape(B, S, D)

def hybrid_layer(x, w_in, b_gate, q_norm_a, k_norm_a, lambda_q1, lambda_k1, lambda_q2, lambda_k2,
                 subln_b, w_proj_a, w_proj_b, w_out, ln1_g, ln1_b, w_query, sub_keys,
                 u_table, v_table, ln2_g, ln2_b, lambda_init, row_tab, col_tab, t_tab):
    B, S, D = x.shape
    proj = x @ w_in
    qa, ka, va, qb, kb, vb, gate_logits = jnp.split(
        proj, [SPLIT_1, SPLIT_2, SPLIT_3, SPLIT_4, SPLIT_5, SPLIT_6], axis=-1)

    qa = apply_axial_rope(rms_norm(qa.reshape(B, S, A_Q_HEADS, HEAD_DIM), q_norm_a), row_tab, col_tab)
    ka = apply_axial_rope(rms_norm(ka.reshape(B, S, A_KV_HEADS, HEAD_DIM), k_norm_a), row_tab, col_tab)
    va = va.reshape(B, S, A_KV_HEADS, HEAD_DIM)
    ya = gqa_attention(qa, ka, va)

    qb = apply_rope(qb.reshape(B, S, B_HEADS * 2, HEAD_DIM), *t_tab).reshape(B, S, B_HEADS, 2, HEAD_DIM)
    kb = apply_rope(kb.reshape(B, S, B_HEADS * 2, HEAD_DIM), *t_tab).reshape(B, S, B_HEADS, 2, HEAD_DIM)
    vb = vb.reshape(B, S, B_HEADS, B_V_DIM)
    lam = (jnp.exp(jnp.sum(lambda_q1.astype(jnp.float32) * lambda_k1.astype(jnp.float32)))
           - jnp.exp(jnp.sum(lambda_q2.astype(jnp.float32) * lambda_k2.astype(jnp.float32)))
           + lambda_init)
    yb = diff_attention(qb, kb, vb, lam, subln_b, lambda_init)

    gates = jax.nn.sigmoid(gate_logits + b_gate).reshape(B, S, 2, D)
    merged = gates[:, :, 0, :] * (ya @ w_proj_a) + gates[:, :, 1, :] * (yb @ w_proj_b)
    h = layer_norm(DN_ALPHA * x + merged @ w_out, ln1_g, ln1_b)

    y = peer_ffn(h, w_query, sub_keys, u_table, v_table)
    return layer_norm(DN_ALPHA * h + y, ln2_g, ln2_b)

def setup_inputs(seed: int = 0) -> dict:
    key = jax.random.key(seed)
    ks = jax.random.split(key, 21)
    L, D = DEPTH, D_MODEL

    def nrm(k, shape, scale):
        return jax.random.normal(k, shape, jnp.float32) * scale

    return {
        'x': nrm(ks[0], (BATCH, SEQ, D), 1.0),
        'w_in': nrm(ks[1], (L, D, IN_COLS), D ** -0.5),
        'b_gate': nrm(ks[2], (L, COLS_GATES), 0.01),
        'q_norm_a': 1.0 + nrm(ks[3], (L, HEAD_DIM), 0.02),
        'k_norm_a': 1.0 + nrm(ks[4], (L, HEAD_DIM), 0.02),
        'lambda_q1': nrm(ks[5], (L, HEAD_DIM), 0.1),
        'lambda_k1': nrm(ks[6], (L, HEAD_DIM), 0.1),
        'lambda_q2': nrm(ks[7], (L, HEAD_DIM), 0.1),
        'lambda_k2': nrm(ks[8], (L, HEAD_DIM), 0.1),
        'subln_b': 1.0 + nrm(ks[9], (L, B_V_DIM), 0.02),
        'w_proj_a': nrm(ks[10], (L, A_WIDTH, D), A_WIDTH ** -0.5 * DN_BETA),
        'w_proj_b': nrm(ks[11], (L, B_WIDTH, D), B_WIDTH ** -0.5 * DN_BETA),
        'w_out': nrm(ks[12], (L, D, D), D ** -0.5 * DN_BETA),
        'ln1_g': 1.0 + nrm(ks[13], (L, D), 0.02),
        'ln1_b': nrm(ks[14], (L, D), 0.01),
        'w_query': nrm(ks[15], (L, D, PEER_HEADS * PEER_QUERY_DIM), D ** -0.5),
        'sub_keys': nrm(ks[16], (L, PEER_HEADS, 2, PEER_N_KEYS, PEER_HALF), PEER_HALF ** -0.5),
        'u_table': nrm(ks[17], (L, PEER_N_EXPERTS, D), D ** -0.5),
        'v_table': nrm(ks[18], (L, PEER_N_EXPERTS, D), DN_BETA),
        'ln2_g': 1.0 + nrm(ks[19], (L, D), 0.02),
        'ln2_b': nrm(ks[20], (L, D), 0.01),
    }

def reference(x, w_in, b_gate, q_norm_a, k_norm_a, lambda_q1, lambda_k1, lambda_q2, lambda_k2,
              subln_b, w_proj_a, w_proj_b, w_out, ln1_g, ln1_b, w_query, sub_keys,
              u_table, v_table, ln2_g, ln2_b):
    S = x.shape[1]
    rows = S // GRID_W
    t_pos = jnp.arange(S, dtype=jnp.int32)
    row_pos = jnp.repeat(jnp.arange(rows, dtype=jnp.int32), GRID_W)
    col_pos = jnp.tile(jnp.arange(GRID_W, dtype=jnp.int32), rows)
    row_tab = rope_tables(row_pos, HEAD_DIM // 2)
    col_tab = rope_tables(col_pos, HEAD_DIM // 2)
    t_tab = rope_tables(t_pos, HEAD_DIM)

    h = x
    for l in range(DEPTH):
        lambda_init = 0.8 - 0.6 * math.exp(-0.3 * l)
        h = hybrid_layer(h, w_in[l], b_gate[l], q_norm_a[l], k_norm_a[l], lambda_q1[l], lambda_k1[l],
                         lambda_q2[l], lambda_k2[l], subln_b[l], w_proj_a[l], w_proj_b[l], w_out[l],
                         ln1_g[l], ln1_b[l], w_query[l], sub_keys[l], u_table[l], v_table[l],
                         ln2_g[l], ln2_b[l], lambda_init, row_tab, col_tab, t_tab)
    return h


_drawn_inputs = setup_inputs


def setup_inputs(seed=0):
    import zlib

    import numpy as np

    out = dict(_drawn_inputs(seed))
    spreads = {}
    factors = {'b_gate': 8.0,
     'q_norm_a': 8.0,
     'k_norm_a': 8.0,
     'lambda_q1': 8.0,
     'lambda_k2': 2.803,
     'subln_b': 3.821,
     'ln2_g': 2.834,
     'ln2_b': 5.898}
    for name, (base, spread) in spreads.items():
        noise = np.random.default_rng([zlib.crc32(name.encode()), seed]).standard_normal(out[name].shape)
        drawn = base * np.exp(spread * noise) if base else spread * noise
        out[name] = __import__('jax').numpy.asarray(drawn.astype(out[name].dtype))
    for name, factor in factors.items():
        out[name] = (out[name] * factor).astype(out[name].dtype)
    return out
```

```python
from contextlib import ExitStack

import numpy as np

import concourse.bass as bass
from concourse import mybir

F32 = mybir.dt.float32
U32 = mybir.dt.uint32
I32 = mybir.dt.int32
ALU = mybir.AluOpType
ACT = mybir.ActivationFunctionType
AX = mybir.AxisListType
ds = bass.ds

P = 128
T, D = 512, 1024
NB = T // P
KD = D // P
HD = 64
AH, BH = 8, 4
NS_A, NS_B = AH, 2 * BH
NSM = NS_A + NS_B
UNITS = AH + BH
KA, KB, VA, VB, QA, QB, GT, COLS = 0, 128, 640, 768, 1280, 1792, 2304, 4352
NCH = 16
CW = COLS // NCH
WI_BUFS = 4
HEADS, NK, TOPK = 8, 128, 16
HI = 2 * HEADS
SLOTS = HEADS * TOPK
RING = 8
BATCH = 4
GROUPS = SLOTS // RING
ALPHA = 2.0 ** 0.25
LAMBDA_INIT = 0.8 - 0.6
EPS, LN_EPS = 1e-6, 1e-5
SCALE = HD ** -0.5
LOWEST = -3.0e38
N_W = 20

DVE_STEPS = 183
FIN_STEPS = 10

STAGES = ["gates", "rope", "attend0", "attend1", "attend2", "attend3", "branches", "merge", "outproj",
          "query0", "query1", "keyscores", "top1", "top2", "choose"]


def build(nc, x_d, xT_d, win_d, wch_d, bgate_d, ln1_d, ln2_d, gains_d, subln_d, lam_d, rope_d, ident_d, iota_d,
          uv_d, out_d):
    with ExitStack() as ctx:
        def sb(name, shape, dt=F32):
            return ctx.enter_context(nc.sbuf_tensor(name, shape, dt))

        def sem(name):
            return ctx.enter_context(nc.semaphore(name))

        bank = [ctx.enter_context(nc.psum_tensor(f"bank{i}", [P, 512], F32)) for i in range(8)]

        ring = sb("ring", [P, RING * 2 * D])
        proj = sb("proj", [P, NB * COLS])
        kT = sb("kT", [P, 5 * T])
        wbuf = sb("wbuf", [P, 2, 2048])
        work = sb("work", [P, 6144])
        h_new = sb("h_new", [P, D])
        h_cur = sb("h_cur", [P, D])
        diag = sb("diag", [P, RING, P])
        ident = sb("ident", [P, P])
        zeros = sb("zeros", [P, P])
        rope = sb("rope", [P, 4, NB * HD])
        gains = sb("gains", [P, 2, HD])
        subln = sb("subln", [P, 2 * HD])
        iota16 = sb("iota16", [P, TOPK])
        lam_e = sb("lam_e", [P, 4])
        neg_lam = sb("neg_lam", [P, 1])
        ss = sb("ss", [P, 8])
        root = sb("root", [P, 8])
        rinv = sb("rinv", [P, 8])
        negmax = sb("negmax", [P, NSM])
        rsum = sb("rsum", [P, NSM])
        rs_inv = sb("rs_inv", [P, NSM])
        stats = sb("stats", [P, 2, 6])
        mv = sb("mv", [P, 2])
        fstats = sb("fstats", [P, 2, 6])
        fmv = sb("fmv", [P, 2])
        froot = sb("froot", [P, 1])
        sv = sb("sv", [P, HI, TOPK])
        si = sb("si", [P, HI, TOPK], U32)
        cv = sb("cv", [P, HEADS, TOPK])
        ci = sb("ci", [P, HEADS, TOPK], U32)
        gsum = sb("gsum", [P, HEADS])
        idx_new = sb("idx_new", [P, SLOTS], I32)
        idx_cur = sb("idx_cur", [P, SLOTS], I32)
        idx_slot = sb("idx_slot", [P, RING], I32)
        gate_new = sb("gate_new", [P, SLOTS])
        gate_cur = sb("gate_cur", [P, SLOTS])
        dots = sb("dots", [P, RING])
        gelu = sb("gelu", [P, RING])

        def uv(k):
            return ring[:, k * 2 * D:(k + 1) * 2 * D]

        xT = ring[:, 0:KD * T].rearrange("p (k t) -> p k t", k=KD)
        wi_flat = [ring[:, KD * T + i * KD * CW:KD * T + (i + 1) * KD * CW] for i in range(WI_BUFS)]
        wi = [piece.rearrange("p (k c) -> p k c", k=KD) for piece in wi_flat]

        def W(i, n=1024):
            return work[:, i * 1024:i * 1024 + n]

        qrot, qT = W(0), W(1).rearrange("p (t q) -> p t q", t=8)
        yT, mT = W(0).rearrange("p (t q) -> p t q", t=8), W(1).rearrange("p (t q) -> p t q", t=8)
        probs = [work[:, 2048 + 512 * i:2560 + 512 * i] for i in range(4)]
        pT = [work[:, 4096 + 512 * i:4608 + 512 * i] for i in range(2)]
        yab = W(5)
        merged, xblk = W(2), W(3)
        hT = W(4).rearrange("p (t q) -> p t q", t=8)
        qqT = W(2, 2048).rearrange("p (t q) -> p t q", t=HI)
        s = W(0, 2048).rearrange("p (t n) -> p t n", t=HI)
        cand = W(2, 2048).rearrange("p (h n) -> p h n", h=HEADS)
        eq1 = W(4, 2048).rearrange("p (k a) -> p k a", a=TOPK)
        eq2 = W(0, 2048).rearrange("p (k a) -> p k a", a=TOPK)
        small = [work[:, 2048 + SLOTS * i:2048 + SLOTS * (i + 1)] for i in range(16)]
        ln2 = W(0, 2048)

        consts_landed = sem("consts_landed")
        zeros_set = sem("zeros_set")
        wi_landed = [sem(f"wi_landed{i}") for i in range(WI_BUFS)]
        tiles_ready = sem("tiles_ready")
        tiles_by_act = sem("tiles_by_act")
        tiles_by_dve = sem("tiles_by_dve")
        key_meansq_ready = sem("key_meansq_ready")
        key_roots_ready = sem("key_roots_ready")
        keys_roped = sem("keys_roped")
        key_tiles_ready = sem("key_tiles_ready")
        kT_ready = sem("kT_ready")
        lam_dots_ready = sem("lam_dots_ready")
        lam_exp_ready = sem("lam_exp_ready")
        setup_step = sem("setup_step")
        w_landed = [sem("w_landed0"), sem("w_landed1")]
        x_landed = sem("x_landed")
        dve_step = sem("dve_step")
        meansq_ready = sem("meansq_ready")
        roots_ready = sem("roots_ready")
        gate_logits_ready = sem("gate_logits_ready")
        gates_ready = sem("gates_ready")
        q_roped = sem("q_roped")
        q_tiles_ready = sem("q_tiles_ready")
        qT_ready = sem("qT_ready")
        scores_ready = sem("scores_ready")
        negmax_ready = sem("negmax_ready")
        probs_ready = sem("probs_ready")
        combined_ready = sem("combined_ready")
        pT_tiles_ready = sem("pT_tiles_ready")
        pT_ready = sem("pT_ready")
        o_ready = sem("o_ready")
        o_taken = sem("o_taken")
        y_ready = sem("y_ready")
        y_tiles_ready = sem("y_tiles_ready")
        yT_ready = sem("yT_ready")
        branch_ready = sem("branch_ready")
        merged_ready = sem("merged_ready")
        m_tiles_ready = sem("m_tiles_ready")
        mT_ready = sem("mT_ready")
        outproj_ready = sem("outproj_ready")
        h_ready = sem("h_ready")
        h_tiles_ready = sem("h_tiles_ready")
        hT_ready = sem("hT_ready")
        query_ready = sem("query_ready")
        qqT_ready = sem("qqT_ready")
        keyscores_ready = sem("keyscores_ready")
        s_ready = sem("s_ready")
        cv_shifted = sem("cv_shifted")
        gate_exp_ready = sem("gate_exp_ready")
        chosen = sem("chosen")
        idx_taken = sem("idx_taken")
        idx_staged = sem("idx_staged")
        slot_free = sem("slot_free")
        waits_passed = sem("waits_passed")
        uv_landed = [sem(f"uv_landed{k}") for k in range(RING)]
        dots_ready = sem("dots_ready")
        gelu_ready = sem("gelu_ready")
        diag_ready = sem("diag_ready")
        y_free = sem("y_free")
        var_ready = sem("var_ready")
        froot_ready = sem("froot_ready")
        fin_step = sem("fin_step")
        out_ready = sem("out_ready")
        out_stored = sem("out_stored")
        ln2_landed = sem("ln2_landed")

        N_CONSTS = 6
        block = ctx.enter_context(nc.Block())

        class Steps:
            def __init__(self, eng, semaphore, base):
                self.eng, self.sem, self.base, self.n = eng, semaphore, base, 0

            def did(self, ins):
                ins.then_inc(self.sem, 1)
                self.n += 1

            def wait(self):
                self.eng.wait_ge(self.sem, self.base + self.n)

            def pass_wait(self):
                self.wait()
                self.eng.sem_inc(waits_passed, 1)

            def alone(self, ins):
                self.did(ins)
                self.wait()

        def schedule(stages):
            out, g = [], 0
            for i, name in enumerate(STAGES):
                out.append(("gather", g, g + 1))
                g += 1
                out.append((name, 0, 0))
            out.append(("gather", g, GROUPS))
            return out

        def run(stages, gather, begin, finish):
            for name in STAGES:
                stages(name, 0)
            begin(0)

            def body(b):
                for name, g0, g1 in schedule(STAGES):
                    if name == "gather":
                        gather(b - 1, g0, g1)
                    else:
                        stages(name, b)
                finish(b - 1)
                begin(b)
            return body

        @block.sync
        def _(sp):
            for i in range(WI_BUFS):
                sp.dma_start(wi_flat[i], win_d[i * P:(i + 1) * P, :]).then_inc(wi_landed[i], 16)
                if i == 0:
                    sp.dma_start(ring[:, 0:KD * T], xT_d).then_inc(wi_landed[0], 16)
            sp.dma_start(ident[:], ident_d).then_inc(consts_landed, 16)
            sp.dma_start(rope[:], rope_d).then_inc(consts_landed, 16)
            sp.dma_start(gains[:].rearrange("p a d -> p (a d)"), gains_d.to_broadcast([P, 2 * HD])).then_inc(consts_landed, 16)
            sp.dma_start(subln[:], subln_d.to_broadcast([P, 2 * HD])).then_inc(consts_landed, 16)
            sp.dma_start(iota16[:], iota_d.to_broadcast([P, TOPK])).then_inc(consts_landed, 16)
            sp.dma_start(W(5, 4 * HD), lam_d.to_broadcast([P, 4 * HD])).then_inc(consts_landed, 16)
            with sp.Fori(1, NCH // WI_BUFS) as it:
                for i in range(WI_BUFS):
                    sp.wait_ge(tiles_ready, ((it - 1) * WI_BUFS + i + 1) * NB)
                    sp.dma_start(wi_flat[i], win_d[ds((it * WI_BUFS + i) * P, P), :]).then_inc(wi_landed[i], 16)

            release = ([(gate_logits_ready, 2, 1), (gate_logits_ready, 2, 2)]
                       + [(branch_ready, 4, n + 1) for n in range(4)]
                       + [(outproj_ready, 4, n + 1) for n in range(4)]
                       + [(h_ready, 1, 1)]
                       + [(query_ready, 8, n + 1) for n in range(8)]
                       + [(keyscores_ready, 4, 4)])
            assert len(release) == N_W

            def stream(b, first):
                for n in range(N_W):
                    if n == 4:
                        sp.wait_ge(y_tiles_ready, 2 * b + 1)
                        sp.dma_start(xblk, x_d[ds(b * P, P), :]).then_inc(x_landed, 16)
                    if n >= 2:
                        semaphore, per_block, count = release[n - 2]
                        sp.wait_ge(semaphore, b * per_block + count)
                    elif not first:
                        semaphore, per_block, count = release[N_W - 2 + n]
                        sp.wait_ge(semaphore, (b - 1) * per_block + count)
                    buf = wbuf[:, n % 2, :]
                    landed = w_landed[n % 2]
                    if n < 2:
                        sp.dma_start(buf[:, 0:D], bgate_d[:, n * D:(n + 1) * D].to_broadcast([P, D])).then_inc(landed, 16)
                    elif n == 10:
                        sp.dma_start(buf, ln1_d.to_broadcast([P, 2 * D])).then_inc(landed, 16)
                    else:
                        sp.dma_start(buf, wch_d[n - 2 - (n > 10)]).then_inc(landed, 16)

            def store(c):
                sp.wait_ge(out_ready, c + 1)
                sp.dma_start(out_d[ds(c * P, P), :], h_cur[:]).then_inc(out_stored, 16)

            stream(0, True)
            with sp.Fori(1, NB) as b:
                stream(b, False)
                sp.wait_ge(chosen, b + 1)
                sp.dma_start(ln2, ln2_d.to_broadcast([P, 2 * D])).then_inc(ln2_landed, 16)
                store(b - 1)
            store(NB - 1)
            sp.wait_ge(out_stored, 16 * NB)

        @block.gpsimd
        def _(pool):
            nc.gpsimd.memset(zeros[:], 0.0).then_inc(zeros_set, 1)
            pool.wait_ge(tiles_ready, NCH * NB)

            def begin(c):
                pool.wait_ge(chosen, c + 1)
                pool.sem_inc(waits_passed, 1)
                nc.gpsimd.tensor_copy(idx_cur[:], idx_new[:]).then_inc(idx_taken, 1)
                pool.wait_ge(idx_taken, c + 1)
                pool.sem_inc(waits_passed, 1)

            def group(G, g):
                for k in range(RING):
                    pool.wait_ge(slot_free, G * RING + k + 1)
                    if k % BATCH == 0:
                        nc.gpsimd.tensor_copy(idx_slot[:, k:k + BATCH],
                                              idx_cur[:, ds(g * RING + k, BATCH)]).then_inc(idx_staged, 1)
                        pool.wait_ge(idx_staged, G * (RING // BATCH) + k // BATCH + 1)
                    pool.sem_inc(waits_passed, 1)
                    nc.gpsimd.indirect_dma_start(
                        out=uv(k), out_offset=None, in_=uv_d,
                        in_offset=bass.IndirectOffsetOnAxis(ap=idx_slot[:, k:k + 1], axis=0)).then_inc(uv_landed[k], 16)

            with pool.Fori(0, NB) as c:
                begin(c)
                with pool.Fori(0, GROUPS) as g:
                    group(c * GROUPS + g, g)

        @block.vector
        def _(dve):
            v = nc.vector
            dve.sem_inc(tiles_by_dve, 4)
            dve.sem_inc(y_free, 1)
            with dve.Fori(0, NCH // WI_BUFS) as it:
                for i in range(WI_BUFS):
                    for tb in (2, 3):
                        dve.wait_ge(tiles_ready, (it * WI_BUFS + i) * NB + tb + 1)
                        v.tensor_copy(proj[:, ds(tb * COLS + (it * WI_BUFS + i) * CW, CW)],
                                      bank[i % 2 * 4 + tb][:, 0:CW]).then_inc(tiles_by_dve, 1)

            setup = Steps(dve, setup_step, 0)

            def rope_tables(kind, b):
                return rope[:, 2 * kind, ds(b * HD, HD)], rope[:, 2 * kind + 1, ds(b * HD, HD)]

            def rotate(steps, out, x, tmp, n, kind, b, last):
                cos, sin = rope_tables(kind, b)
                parts = 2 if kind == 0 else 1
                half = HD // parts // 2
                m = n * parts
                hv = "p (m s d) -> p m s d"
                x4 = x.rearrange(hv, m=m, s=2)
                t4 = tmp.rearrange(hv, m=m, s=2)
                s4 = sin.rearrange("p (a s d) -> p a s d", a=parts, s=2)
                for side in range(2):
                    if kind == 0:
                        o_ap = t4[:, :, side, :].rearrange("p (n a) d -> p n a d", a=2)
                        x_ap = x4[:, :, 1 - side, :].rearrange("p (n a) d -> p n a d", a=2)
                        s_ap = s4[:, :, side, :].unsqueeze(1).to_broadcast([P, n, 2, half])
                    else:
                        o_ap, x_ap = t4[:, :, side, :], x4[:, :, 1 - side, :]
                        s_ap = s4[:, 0, side, :].unsqueeze(1).to_broadcast([P, n, half])
                    steps.did(v.tensor_tensor(o_ap, x_ap, s_ap, ALU.mult))
                hx = "p (n d) -> p n d"
                steps.alone(v.tensor_tensor(out.rearrange(hx, n=n), x.rearrange(hx, n=n),
                                            cos.unsqueeze(1).to_broadcast([P, n, HD]), ALU.mult))
                ins = v.tensor_tensor(out, out, tmp, ALU.add)
                if last is None:
                    steps.did(ins)
                else:
                    ins.then_inc(last, 1)

            dve.wait_ge(tiles_by_act, 4 + 2 * NCH)
            dve.wait_ge(tiles_by_dve, 4 + 2 * NCH)
            dve.wait_ge(consts_landed, 16 * N_CONSTS)
            krot = work[:, 0:2560]
            sq, ktmp, ky = work[:, 2560:3072], work[:, 3072:3584], work[:, 3584:4096]
            ka = proj[:].rearrange("p (b c) -> p b c", b=NB)[:, :, KA:KA + 2 * HD]
            setup.alone(v.tensor_tensor(sq.rearrange("p (b c) -> p b c", b=NB), ka, ka, ALU.mult))
            setup.alone(v.tensor_reduce(ss[:], sq.rearrange("p (n d) -> p n d", d=HD), AX.X, ALU.add))
            v.tensor_scalar(ss[:], ss[:], 1.0 / HD, EPS, ALU.mult, ALU.add).then_inc(key_meansq_ready, 1)
            lam = W(5, 4 * HD).rearrange("p (a d) -> p a d", a=4)
            lam_prod = work[:, 5120 + 4 * HD:5120 + 6 * HD].rearrange("p (a d) -> p a d", a=2)
            for a in range(2):
                setup.did(v.tensor_tensor(lam_prod[:, a, :], lam[:, 2 * a, :], lam[:, 2 * a + 1, :], ALU.mult))
            setup.wait()
            v.tensor_reduce(lam_e[:, 0:2], lam_prod, AX.X, ALU.add).then_inc(lam_dots_ready, 1)
            setup.did(v.tensor_scalar(subln[:], subln[:], 1.0 - LAMBDA_INIT, None, ALU.mult))
            dve.wait_ge(lam_exp_ready, 1)
            setup.alone(v.tensor_tensor(neg_lam[:], lam_e[:, 3:4], lam_e[:, 2:3], ALU.subtract))
            setup.alone(v.tensor_scalar(neg_lam[:], neg_lam[:], -LAMBDA_INIT, None, ALU.add))
            dve.wait_ge(key_roots_ready, 1)
            setup.alone(v.reciprocal(rinv[:], root[:]))
            for kb in range(NB):
                base = kb * COLS
                k3 = proj[:, base + KA:base + KA + 2 * HD].rearrange("p (n d) -> p n d", n=2)
                y3 = ky[:, 0:2 * HD].rearrange("p (n d) -> p n d", n=2)
                setup.alone(v.tensor_tensor(y3, k3, rinv[:, 2 * kb:2 * kb + 2].unsqueeze(2).to_broadcast([P, 2, HD]),
                                            ALU.mult))
                setup.alone(v.tensor_tensor(y3, y3, gains[:, 1, :].unsqueeze(1).to_broadcast([P, 2, HD]), ALU.mult))
                out = krot[:, kb * 640:(kb + 1) * 640]
                rotate(setup, out[:, 0:128], ky[:, 0:128], ktmp[:, 0:128], 2, 0, kb, None)
                setup.wait()
                rotate(setup, out[:, 128:640], proj[:, base + KB:base + KB + 512], ktmp, 8, 1, kb, keys_roped)
                setup.wait()

            def root_of(steps, b, which, src, n, scale, eps):
                v.tensor_scalar(ss[:, 0:n], src, scale, eps, ALU.mult, ALU.add).then_inc(meansq_ready, 1)
                dve.wait_ge(roots_ready, 3 * b + which + 1)
                steps.alone(v.reciprocal(rinv[:, 0:n], root[:, 0:n]))

            hold = {}

            def landed(b, n):
                dve.wait_ge(w_landed[n % 2], 16 * (b * (N_W // 2) + n // 2 + 1))

            def top16(steps, vals, best, index, rows):
                for j in rows:
                    steps.did(v.max(best(j)[:, 0:8], vals(j)))
                steps.pass_wait()
                for j in rows:
                    steps.did(v.max_index(index(j)[:, 0:8], best(j)[:, 0:8], vals(j)))
                for j in rows:
                    steps.did(v.match_replace(vals(j), best(j)[:, 0:8], vals(j), LOWEST))
                steps.pass_wait()
                for j in rows:
                    steps.did(v.max(best(j)[:, 8:16], vals(j)))
                steps.pass_wait()
                for j in rows:
                    steps.did(v.max_index(index(j)[:, 8:16], best(j)[:, 8:16], vals(j)))

            def attend(b, u0, u1):
                for u in range(u0, u1):
                    sms = [u] if u < AH else [AH + 2 * (u - AH), AH + 2 * (u - AH) + 1]
                    if u < UNITS:
                        for m in sms:
                            dve.wait_ge(scores_ready, b * NSM + m + 1)
                            v.tensor_reduce(negmax[:, m:m + 1], bank[2 + m % 2][:], AX.X, ALU.max,
                                            negate=True).then_inc(negmax_ready, 1)
                        dve.wait_ge(probs_ready, b * NSM + sms[-1] + 1)
                        steps = hold["steps"]
                        steps.alone(v.reciprocal(rs_inv[:, sms[0]:sms[-1] + 1], rsum[:, sms[0]:sms[-1] + 1]))
                        if u >= AH:
                            steps.did(v.tensor_scalar(probs[sms[0] % 4], probs[sms[0] % 4],
                                                      rs_inv[:, sms[0]:sms[0] + 1], None, ALU.mult))
                            steps.alone(v.tensor_scalar(rs_inv[:, sms[1]:sms[1] + 1], rs_inv[:, sms[1]:sms[1] + 1],
                                                        neg_lam[:, 0:1], None, ALU.mult))
                            v.scalar_tensor_tensor(probs[sms[0] % 4], probs[sms[1] % 4],
                                                   rs_inv[:, sms[1]:sms[1] + 1], probs[sms[0] % 4],
                                                   ALU.mult, ALU.add).then_inc(combined_ready, 1)
                    if u >= 1:
                        w = u - 1
                        dve.wait_ge(o_ready, b * UNITS + w + 1)
                        if w < AH:
                            v.tensor_scalar(yab[:, w * HD:(w + 1) * HD], bank[6 + w % 2][:, 0:HD],
                                            rs_inv[:, w:w + 1], None, ALU.mult).then_inc(o_taken, 1)
                        else:
                            c0 = AH * HD + (w - AH) * 2 * HD
                            v.tensor_copy(yab[:, c0:c0 + 2 * HD], bank[6 + w % 2][:, 0:2 * HD]).then_inc(o_taken, 1)

            def stages(name, b):
                if name == "gates":
                    hold["steps"] = Steps(dve, dve_step, b * DVE_STEPS)
                steps = hold["steps"]
                if name == "gates":
                    for n in range(2):
                        landed(b, n)
                        g = proj[:, ds(b * COLS + GT + n * D, D)]
                        v.tensor_tensor(g, g, wbuf[:, n, 0:D], ALU.add).then_inc(gate_logits_ready, 1)
                elif name == "rope":
                    if isinstance(b, int):
                        dve.wait_ge(keys_roped, NB)
                        dve.wait_ge(key_tiles_ready, 5)
                    q = proj[:, ds(b * COLS + QA, 512)]
                    sq, qy, tmp = W(2, 512), W(3, 512), W(4, 512)
                    hx = "p (n d) -> p n d"
                    steps.alone(v.tensor_tensor(sq, q, q, ALU.mult))
                    steps.alone(v.tensor_reduce(ss[:], sq.rearrange(hx, n=AH), AX.X, ALU.add))
                    root_of(steps, b, 0, ss[:], AH, 1.0 / HD, EPS)
                    steps.alone(v.tensor_tensor(qy.rearrange(hx, n=AH), q.rearrange(hx, n=AH),
                                                rinv[:].unsqueeze(2).to_broadcast([P, AH, HD]), ALU.mult))
                    steps.alone(v.tensor_tensor(qy.rearrange(hx, n=AH), qy.rearrange(hx, n=AH),
                                                gains[:, 0, :].unsqueeze(1).to_broadcast([P, AH, HD]), ALU.mult))
                    rotate(steps, qrot[:, 0:512], qy, tmp, AH, 0, b, q_roped)
                    rotate(steps, qrot[:, 512:1024], proj[:, ds(b * COLS + QB, 512)], W(5, 512), NS_B, 1, b, q_roped)
                elif name.startswith("attend"):
                    n = int(name[-1])
                    attend(b, 3 * n, 3 * n + 3 + (n == 3))
                elif name == "branches":
                    dve.wait_ge(o_taken, (b + 1) * UNITS)
                    yb = yab[:, 512:1024]
                    sq = W(3, 512)
                    hx = "p (n d) -> p n d"
                    steps.alone(v.tensor_tensor(sq, yb, yb, ALU.mult))
                    steps.alone(v.tensor_reduce(ss[:, 0:BH], sq.rearrange(hx, n=BH), AX.X, ALU.add))
                    root_of(steps, b, 1, ss[:, 0:BH], BH, 1.0 / (2 * HD), EPS)
                    steps.alone(v.tensor_tensor(yb.rearrange(hx, n=BH), yb.rearrange(hx, n=BH),
                                                rinv[:, 0:BH].unsqueeze(2).to_broadcast([P, BH, 2 * HD]), ALU.mult))
                    v.tensor_tensor(yb.rearrange(hx, n=BH), yb.rearrange(hx, n=BH),
                                    subln[:].unsqueeze(1).to_broadcast([P, BH, 2 * HD]), ALU.mult).then_inc(y_ready, 1)
                elif name == "merge":
                    dve.wait_ge(gates_ready, 2 * b + 2)
                    for n in range(2):
                        gA = proj[:, ds(b * COLS + GT + n * 512, 512)]
                        gB = proj[:, ds(b * COLS + GT + D + n * 512, 512)]
                        m, t = merged[:, n * 512:(n + 1) * 512], yab[:, n * 512:(n + 1) * 512]
                        dve.wait_ge(branch_ready, 4 * b + 2 * n + 1)
                        steps.did(v.tensor_tensor(m, gA, bank[4 + 2 * n][:], ALU.mult))
                        dve.wait_ge(branch_ready, 4 * b + 2 * n + 2)
                        steps.alone(v.tensor_tensor(t, gB, bank[5 + 2 * n][:], ALU.mult))
                        v.tensor_tensor(m, m, t, ALU.add).then_inc(merged_ready, 1)
                elif name == "outproj":
                    dve.wait_ge(x_landed, 16 * (b + 1))
                    for n in range(2):
                        c = slice(n * 512, (n + 1) * 512)
                        dve.wait_ge(outproj_ready, 4 * b + 2 * n + 2)
                        steps.alone(v.scalar_tensor_tensor(h_new[:, c], xblk[:, c], ALPHA, bank[4 + n][:],
                                                           ALU.mult, ALU.add))
                        steps.did(v.bn_stats(stats[:, n, :], h_new[:, c]))
                    steps.pass_wait()
                    steps.alone(v.bn_aggr(mv[:], stats[:]))
                    root_of(steps, b, 2, mv[:, 1:2], 1, 1.0, LN_EPS)
                    steps.alone(v.tensor_scalar(h_new[:], h_new[:], mv[:, 0:1], rinv[:, 0:1], ALU.subtract, ALU.mult))
                    landed(b, 10)
                    steps.alone(v.tensor_tensor(h_new[:], h_new[:], wbuf[:, 0, 0:D], ALU.mult))
                    v.tensor_tensor(h_new[:], h_new[:], wbuf[:, 0, D:2 * D], ALU.add).then_inc(h_ready, 1)
                elif name in ("top1", "top2"):
                    half = int(name[-1]) - 1
                    dve.wait_ge(s_ready, 4 * b + 2 * half + 2)
                    dve.sem_inc(waits_passed, 1)
                    top16(steps, lambda j: s[:, j, :], lambda j: sv[:, j, :], lambda j: si[:, j, :],
                          range(8 * half, 8 * half + 8))
                    if half:
                        steps.wait()
                        sv4 = sv[:].rearrange("p (h i) k -> p h i k", i=2)
                        steps.alone(v.tensor_tensor(
                            cand.rearrange("p h (a b) -> p h a b", a=TOPK),
                            sv4[:, :, 0, :].unsqueeze(3).to_broadcast([P, HEADS, TOPK, TOPK]),
                            sv4[:, :, 1, :].unsqueeze(2).to_broadcast([P, HEADS, TOPK, TOPK]), ALU.add))
                elif name == "choose":
                    steps.pass_wait()
                    top16(steps, lambda j: cand[:, j, :], lambda j: cv[:, j, :], lambda j: ci[:, j, :], range(HEADS))
                    steps.wait()
                    steps.alone(v.tensor_copy(gsum[:], cv[:, :, 0]))
                    v.tensor_tensor(cv[:], cv[:], gsum[:].unsqueeze(2).to_broadcast([P, HEADS, TOPK]),
                                    ALU.subtract).then_inc(cv_shifted, 1)
                    cif = ci[:].rearrange("p h k -> p (h k)")
                    pa, pb = small[0].bitcast(U32), small[1].bitcast(U32)
                    paf, pbf, e1, e2 = small[2], small[3], small[4], small[5]
                    sif = work[:, 2048 + 8 * SLOTS:2048 + 10 * SLOTS].rearrange("p (h i k) -> p h i k", h=HEADS, i=2)
                    steps.did(v.tensor_scalar(pa, cif, 4, None, ALU.logical_shift_right))
                    steps.did(v.tensor_scalar(pb, cif, TOPK - 1, None, ALU.bitwise_and))
                    steps.alone(v.tensor_copy(sif, si[:].rearrange("p (h i) k -> p h i k", i=2)))
                    steps.did(v.tensor_copy(paf, pa))
                    steps.alone(v.tensor_copy(pbf, pb))
                    for pf, eq, e, i in ((paf, eq1, e1, 0), (pbf, eq2, e2, 1)):
                        steps.alone(v.tensor_tensor(eq, pf.unsqueeze(2).to_broadcast([P, SLOTS, TOPK]),
                                                    iota16[:].unsqueeze(1).to_broadcast([P, SLOTS, TOPK]), ALU.is_equal))
                        eq4 = eq.rearrange("p (h k) a -> p h k a", h=HEADS)
                        steps.alone(v.tensor_tensor(eq4, eq4, sif[:, :, i, :].unsqueeze(2)
                                                    .to_broadcast([P, HEADS, TOPK, TOPK]), ALU.mult))
                        steps.alone(v.tensor_reduce(e, eq, AX.X, ALU.add))
                    dve.wait_ge(gate_exp_ready, b + 1)
                    steps.alone(v.tensor_reduce(gsum[:], cv[:], AX.X, ALU.add))
                    steps.alone(v.reciprocal(gsum[:], gsum[:]))
                    steps.did(v.tensor_tensor(gate_new[:].rearrange("p (h k) -> p h k", h=HEADS), cv[:],
                                              gsum[:].unsqueeze(2).to_broadcast([P, HEADS, TOPK]), ALU.mult))
                    if not isinstance(b, int):
                        dve.wait_ge(idx_taken, b)
                    v.scalar_tensor_tensor(idx_new[:], e1, float(NK), e2, ALU.mult, ALU.add).then_inc(chosen, 1)
                    assert steps.n == DVE_STEPS, steps.n

            def group(c, g):
                G = c * GROUPS + g
                for bt in range(RING // BATCH):
                    for k in range(bt * BATCH, (bt + 1) * BATCH):
                        dve.wait_ge(uv_landed[k], (G + 1) * 16)
                        u = uv(k)[:, 0:D]
                        ins = v.tensor_tensor_reduce(out=u, in0=u, in1=h_cur[:], scale=1.0, scalar=0.0, op0=ALU.mult,
                                                     op1=ALU.add, accum_out=dots[:, k:k + 1])
                    ins.then_inc(dots_ready, 1)
                    dve.wait_ge(gelu_ready, G * (RING // BATCH) + bt + 1)
                    dve.wait_ge(slot_free, G * RING + (bt + 1) * BATCH)
                    for k in range(bt * BATCH, (bt + 1) * BATCH):
                        v.tensor_scalar(diag[:, k, :], ident[:], gelu[:, k:k + 1],
                                        gate_cur[:, ds(g * RING + k, 1)], ALU.mult, ALU.mult).then_inc(diag_ready, 1)

            def gather(c, g0, g1):
                if g1 - g0 > 1:
                    with dve.Fori(g0, g1) as g:
                        group(c, g)
                elif g1 > g0:
                    group(c, g0)

            def begin(b):
                steps = Steps(dve, fin_step, b * FIN_STEPS)
                dve.wait_ge(h_ready, b + 1)
                dve.wait_ge(dve_step, (b + 1) * DVE_STEPS)
                if not isinstance(b, int):
                    dve.wait_ge(out_stored, b * 16)
                steps.did(v.tensor_copy(gate_cur[:], gate_new[:]))
                steps.alone(v.tensor_copy(h_cur[:], h_new[:]))
                assert steps.n == 2

            def finish(c):
                steps = Steps(dve, fin_step, c * FIN_STEPS)
                steps.n = 2
                dve.wait_ge(slot_free, (c + 1) * SLOTS + RING)
                for n in range(2):
                    col = slice(n * 512, (n + 1) * 512)
                    steps.did(v.scalar_tensor_tensor(h_cur[:, col], h_cur[:, col], ALPHA, bank[n][:], ALU.mult, ALU.add))
                steps.wait()
                v.bn_stats(fstats[:, 0, :], h_cur[:, 0:512]).then_inc(y_free, 1)
                steps.did(v.bn_stats(fstats[:, 1, :], h_cur[:, 512:1024]))
                steps.pass_wait()
                steps.alone(v.bn_aggr(fmv[:], fstats[:]))
                steps.did(v.tensor_scalar(fmv[:, 1:2], fmv[:, 1:2], LN_EPS, None, ALU.add))
                steps.eng.wait_ge(froot_ready, c + 1)
                steps.alone(v.reciprocal(froot[:], froot[:]))
                steps.alone(v.tensor_scalar(h_cur[:], h_cur[:], fmv[:, 0:1], froot[:, 0:1], ALU.subtract, ALU.mult))
                dve.wait_ge(ln2_landed, 16 * (NB - 1) if isinstance(c, int) else (c + 1) * 16)
                steps.alone(v.tensor_tensor(h_cur[:], h_cur[:], ln2[:, 0:D], ALU.mult))
                v.tensor_tensor(h_cur[:], h_cur[:], ln2[:, D:2 * D], ALU.add).then_inc(out_ready, 1)
                assert steps.n == FIN_STEPS, steps.n

            body = run(stages, gather, begin, finish)
            with dve.Fori(1, NB) as b:
                body(b)
            gather(NB - 1, 0, GROUPS)
            finish(NB - 1)

        @block.scalar
        def _(act):
            a = nc.scalar
            act.sem_inc(tiles_by_act, 4)
            with act.Fori(0, NCH // WI_BUFS) as it:
                for i in range(WI_BUFS):
                    for tb in (0, 1):
                        act.wait_ge(tiles_ready, (it * WI_BUFS + i) * NB + tb + 1)
                        a.activation(proj[:, ds(tb * COLS + (it * WI_BUFS + i) * CW, CW)],
                                     bank[i % 2 * 4 + tb][:, 0:CW], ACT.Copy).then_inc(tiles_by_act, 1)
            act.wait_ge(lam_dots_ready, 1)
            a.activation(lam_e[:, 2:4], lam_e[:, 0:2], ACT.Exp).then_inc(lam_exp_ready, 1)
            act.wait_ge(key_meansq_ready, 1)
            a.activation(root[:], ss[:], ACT.Sqrt).then_inc(key_roots_ready, 1)
            for t in range(5):
                act.wait_ge(key_tiles_ready, t + 1)
                a.activation(kT[:, t * T:(t + 1) * T], bank[2 + t][:], ACT.Copy).then_inc(kT_ready, 1)

            def take_root(b, which, n):
                act.wait_ge(meansq_ready, 3 * b + which + 1)
                a.activation(root[:, 0:n], ss[:, 0:n], ACT.Sqrt).then_inc(roots_ready, 1)

            def two_tiles(b, asked, done, dst, scale=1.0):
                for n in range(2):
                    act.wait_ge(asked, 2 * b + n + 1)
                    a.activation(dst[:, 4 * n:4 * n + 4, :].rearrange("p t q -> p (t q)"), bank[2 + n][:],
                                 ACT.Copy, scale=scale).then_inc(done, 1)

            def attend(b, u0, u1):
                for u in range(u0, u1):
                    if u < UNITS:
                        for m in ([u] if u < AH else [AH + 2 * (u - AH), AH + 2 * (u - AH) + 1]):
                            act.wait_ge(negmax_ready, b * NSM + m + 1)
                            a.activation(probs[m % 4], bank[2 + m % 2][:], ACT.Exp, bias=negmax[:, m:m + 1],
                                         accum_out=rsum[:, m:m + 1]).then_inc(probs_ready, 1)
                    if u >= 1:
                        act.wait_ge(pT_tiles_ready, b * UNITS + u)
                        a.activation(pT[(u - 1) % 2], bank[4 + (u - 1) % 2][:], ACT.Copy).then_inc(pT_ready, 1)

            def stages(name, b):
                if name == "gates":
                    for n in range(2):
                        act.wait_ge(gate_logits_ready, 2 * b + n + 1)
                        g = proj[:, ds(b * COLS + GT + n * D, D)]
                        a.activation(g, g, ACT.Sigmoid).then_inc(gates_ready, 1)
                elif name == "rope":
                    take_root(b, 0, AH)
                    two_tiles(b, q_tiles_ready, qT_ready, qT, SCALE)
                elif name.startswith("attend"):
                    n = int(name[-1])
                    attend(b, 3 * n, 3 * n + 3 + (n == 3))
                elif name == "branches":
                    take_root(b, 1, BH)
                    two_tiles(b, y_tiles_ready, yT_ready, yT)
                elif name == "merge":
                    two_tiles(b, m_tiles_ready, mT_ready, mT)
                elif name == "outproj":
                    take_root(b, 2, 1)
                    two_tiles(b, h_tiles_ready, hT_ready, hT)
                elif name in ("query0", "query1"):
                    for n in range(2 * int(name[-1]), 2 * int(name[-1]) + 2):
                        act.wait_ge(query_ready, 8 * b + 2 * n + 2)
                        a.activation(qqT[:, 4 * n:4 * n + 4, :].rearrange("p t q -> p (t q)"), bank[4 + n][:],
                                     ACT.Copy).then_inc(qqT_ready, 1)
                elif name == "keyscores":
                    for n in range(4):
                        act.wait_ge(keyscores_ready, 4 * b + n + 1)
                        a.activation(s[:, 4 * n:4 * n + 4, :].rearrange("p t q -> p (t q)"), bank[2 + n][:],
                                     ACT.Copy).then_inc(s_ready, 1)
                elif name == "choose":
                    act.wait_ge(cv_shifted, b + 1)
                    a.activation(cv[:], cv[:], ACT.Exp).then_inc(gate_exp_ready, 1)

            def group(c, g):
                for bt in range(RING // BATCH):
                    act.wait_ge(dots_ready, (c * GROUPS + g) * (RING // BATCH) + bt + 1)
                    a.activation(gelu[:, bt * BATCH:(bt + 1) * BATCH], dots[:, bt * BATCH:(bt + 1) * BATCH],
                                 ACT.Gelu).then_inc(gelu_ready, 1)

            def gather(c, g0, g1):
                if g1 - g0 > 1:
                    with act.Fori(g0, g1) as g:
                        group(c, g)
                elif g1 > g0:
                    group(c, g0)

            def finish(c):
                act.wait_ge(fin_step, c * FIN_STEPS + 7)
                a.activation(froot[:], fmv[:, 1:2], ACT.Sqrt).then_inc(froot_ready, 1)

            body = run(stages, gather, lambda b: None, finish)
            with act.Fori(1, NB) as b:
                body(b)
            gather(NB - 1, 0, GROUPS)
            finish(NB - 1)

        @block.tensor
        def _(pe):
            t_ = nc.tensor
            pe.sem_inc(slot_free, RING)
            pe.wait_ge(wi_landed[0], 32)
            with pe.Fori(0, NCH // WI_BUFS) as it:
                for i in range(WI_BUFS):
                    pe.wait_ge(wi_landed[i], it * 16 + (32 if i == 0 else 16))
                    for tb in range(NB):
                        pe.wait_ge(tiles_by_act if tb < 2 else tiles_by_dve, (it * WI_BUFS + i) * 2 + tb % 2 + 1)
                        for k in range(KD):
                            ins = t_.matmul(bank[i % 2 * 4 + tb][:, 0:CW], xT[:, k, tb * P:(tb + 1) * P], wi[i][:, k, :],
                                            start=(k == 0), stop=(k == KD - 1))
                        ins.then_inc(tiles_ready, 1)

            pe.wait_ge(keys_roped, NB)
            krot = work[:, 0:2560]
            for t in range(5):
                for kb in range(NB):
                    ins = t_.transpose(bank[2 + t][:, kb * P:(kb + 1) * P],
                                       krot[:, kb * 640 + t * P:kb * 640 + (t + 1) * P], ident[:])
                ins.then_inc(key_tiles_ready, 1)
            pe.wait_ge(kT_ready, 5)

            def landed(b, n):
                pe.wait_ge(w_landed[n % 2], 16 * (b * (N_W // 2) + n // 2 + 1))

            def two_tiles(src, done):
                for n in range(2):
                    for j in range(4):
                        ins = t_.transpose(bank[2 + n][:, j * P:(j + 1) * P], src[:, (4 * n + j) * P:(4 * n + j + 1) * P],
                                           ident[:])
                    ins.then_inc(done, 1)

            def scores(b, u):
                for m in ([u] if u < AH else [AH + 2 * (u - AH), AH + 2 * (u - AH) + 1]):
                    if m == 0:
                        pe.wait_ge(qT_ready, 2 * b + 2)
                    if m >= 2:
                        pe.wait_ge(probs_ready, b * NSM + m - 1)
                    if u < AH:
                        g, tile, ktile = u // 4, u % 4, 0
                    else:
                        g, tile, ktile = m % 2, 4 + (u - AH), 1 + (u - AH)
                    rows = slice(g * HD, (g + 1) * HD)
                    t_.matmul(bank[2 + m % 2][:], qT[rows, tile, :], kT[rows, ktile * T:(ktile + 1) * T],
                              start=True, stop=True).then_inc(scores_ready, 1)

            def attend(b, u0, u1):
                if u0 == 0:
                    scores(b, 0)
                for u in range(u0, u1):
                    if u + 1 < UNITS:
                        scores(b, u + 1)
                    if u < UNITS:
                        if u < AH:
                            pe.wait_ge(probs_ready, b * NSM + u + 1)
                            pu = probs[u % 4]
                        else:
                            pe.wait_ge(combined_ready, b * BH + u - AH + 1)
                            pu = probs[2 * (u - AH) % 4]
                        for j in range(NB):
                            ins = t_.transpose(bank[4 + u % 2][:, j * P:(j + 1) * P], pu[:, j * P:(j + 1) * P], ident[:])
                        ins.then_inc(pT_tiles_ready, 1)
                    if u >= 1:
                        w = u - 1
                        pe.wait_ge(pT_ready, b * UNITS + w + 1)
                        if w >= 2:
                            pe.wait_ge(o_taken, b * UNITS + w - 1)
                        width = HD if w < AH else 2 * HD
                        for kc in range(NB):
                            c0 = kc * COLS + (VA + (w // 4) * HD if w < AH else VB + (w - AH) * 2 * HD)
                            ins = t_.matmul(bank[6 + w % 2][:, 0:width], pT[w % 2][:, kc * P:(kc + 1) * P],
                                            proj[:, c0:c0 + width], start=(kc == 0), stop=(kc == NB - 1))
                        ins.then_inc(o_ready, 1)

            def stages(name, b):
                if name == "rope":
                    pe.wait_ge(q_roped, 2 * b + 2)
                    if not isinstance(b, int):
                        pe.wait_ge(s_ready, 4 * b)
                    two_tiles(qrot, q_tiles_ready)
                elif name.startswith("attend"):
                    n = int(name[-1])
                    attend(b, 3 * n, 3 * n + 3 + (n == 3))
                elif name == "branches":
                    pe.wait_ge(y_ready, b + 1)
                    two_tiles(yab, y_tiles_ready)
                    pe.wait_ge(yT_ready, 2 * b + 2)
                    for n in range(4):
                        landed(b, 2 + n)
                        w = wbuf[:, n % 2, :].rearrange("p (k c) -> p k c", k=4)
                        for k in range(4):
                            ins = t_.matmul(bank[4 + n][:], yT[:, 4 * (n % 2) + k, :], w[:, k, :],
                                            start=(k == 0), stop=(k == 3))
                        ins.then_inc(branch_ready, 1)
                elif name == "merge":
                    pe.wait_ge(merged_ready, 2 * b + 2)
                    two_tiles(merged, m_tiles_ready)
                elif name == "outproj":
                    pe.wait_ge(mT_ready, 2 * b + 2)
                    for n in range(4):
                        landed(b, 6 + n)
                        w = wbuf[:, n % 2, :].rearrange("p (k c) -> p k c", k=KD)
                        for k in range(KD):
                            ins = t_.matmul(bank[4 + n // 2][:, n % 2 * 256:n % 2 * 256 + 256], mT[:, k, :], w[:, k, :],
                                            start=(k == 0), stop=(k == KD - 1))
                        ins.then_inc(outproj_ready, 1)
                    pe.wait_ge(h_ready, b + 1)
                    two_tiles(h_new, h_tiles_ready)
                elif name in ("query0", "query1"):
                    pe.wait_ge(hT_ready, 2 * b + 2)
                    for q in range(4 * int(name[-1]), 4 * int(name[-1]) + 4):
                        landed(b, 11 + q)
                        w = wbuf[:, (11 + q) % 2, :].rearrange("p (k c) -> p k c", k=KD)
                        for j in range(2):
                            ct = 2 * q + j
                            for k in range(KD):
                                ins = t_.matmul(bank[4 + ct // 4][:, ct % 4 * P:ct % 4 * P + P], w[:, k, j * P:(j + 1) * P],
                                                hT[:, k, :], start=(k == 0), stop=(k == KD - 1))
                        ins.then_inc(query_ready, 1)
                elif name == "keyscores":
                    landed(b, 19)
                    keys = wbuf[:, 1, :].rearrange("p (t n) -> p t n", t=HI)
                    pe.wait_ge(qqT_ready, 4 * b + 4)
                    for hi in range(HI):
                        ins = t_.matmul(bank[2 + hi // 4][:, hi % 4 * P:hi % 4 * P + P], qqT[:, hi, :], keys[:, hi, :],
                                        start=True, stop=True)
                        if hi % 4 == 3:
                            ins.then_inc(keyscores_ready, 1)

            def clear(c):
                pe.wait_ge(y_free, c + 1)
                for n in range(2):
                    t_.matmul(bank[n][:, 0:2], zeros[:], zeros[:, 0:2], start=True, stop=False, skip_group_check=True)

            def group(c, g):
                G = c * GROUPS + g
                for k in range(RING):
                    pe.wait_ge(diag_ready, G * RING + k + 1)
                    for n in range(2):
                        ins = t_.matmul(bank[n][:], diag[:, k, :], uv(k)[:, D + n * 512:D + (n + 1) * 512],
                                        start=False, stop=False, skip_group_check=True)
                    ins.then_inc(slot_free, 1)

            def gather(c, g0, g1):
                if g0 == 0:
                    clear(c)
                if g1 - g0 > 1:
                    with pe.Fori(g0, g1) as g:
                        group(c, g)
                elif g1 > g0:
                    group(c, g0)

            pe.wait_ge(zeros_set, 1)
            body = run(stages, gather, lambda b: None, lambda c: None)
            with pe.Fori(1, NB) as b:
                body(b)
            gather(NB - 1, 0, GROUPS)


def rope_table():
    def table(pos, dim):
        freqs = np.float32(10000.0) ** (-np.arange(0, dim, 2, dtype=np.float32) / np.float32(dim))
        ang = pos.astype(np.float32)[:, None] * freqs[None, :]
        cos, sin = np.cos(ang), np.sin(ang)
        return np.concatenate([cos, cos], 1), np.concatenate([-sin, sin], 1)

    pos = np.arange(T)
    row, col, seq = table(pos // 64, HD // 2), table(pos % 64, HD // 2), table(pos, HD)
    a = [np.concatenate([row[i], col[i]], 1) for i in range(2)]
    out = np.stack([a[0], a[1], seq[0], seq[1]]).astype(np.float32)
    return np.ascontiguousarray(out.reshape(4, NB, P, HD).transpose(2, 0, 1, 3).reshape(P, 4, NB * HD))


def kernel(**inputs):
    import concourse.bacc as bacc
    from concourse.bass_utils import run_bass_kernel_spmd

    f = {k: np.asarray(a) for k, a in inputs.items()}
    x = f["x"][0]
    w_in = f["w_in"][0]
    qa = w_in[:, 0:512].reshape(D, 2, 4, HD).transpose(0, 2, 1, 3).reshape(D, 512)
    w_in = np.concatenate([w_in[:, 512:640], w_in[:, 1280:1792], w_in[:, 640:768], w_in[:, 1792:2304], qa,
                           w_in[:, 768:1280], w_in[:, 2304:]], axis=1)
    w_in = w_in.reshape(KD, P, NCH, CW).transpose(2, 1, 0, 3).reshape(NCH * P, KD * CW)

    def pieces(w, width):
        rows, cols = w.shape
        return list(w.reshape(rows // P, P, cols // width, width).transpose(2, 1, 0, 3).reshape(-1, P, 2048))

    a, b = pieces(f["w_proj_a"][0], 512), pieces(f["w_proj_b"][0], 512)
    keys = f["sub_keys"][0].transpose(3, 0, 1, 2).reshape(P, HI * NK)
    wch = np.stack([a[0], b[0], a[1], b[1]] + pieces(f["w_out"][0], 256) + pieces(f["w_query"][0], 256) + [keys])
    arrays = {
        "x": x,
        "xT": x.T.reshape(KD, P, T).transpose(1, 0, 2).reshape(P, KD * T),
        "w_in": w_in,
        "w_chunks": wch,
        "b_gate": f["b_gate"],
        "ln1": np.concatenate([f["ln1_g"], f["ln1_b"]], axis=1),
        "ln2": np.concatenate([f["ln2_g"], f["ln2_b"]], axis=1),
        "gains": np.concatenate([f["q_norm_a"], f["k_norm_a"]], axis=1),
        "subln": f["subln_b"],
        "lambdas": np.concatenate([f["lambda_q1"], f["lambda_k1"], f["lambda_q2"], f["lambda_k2"]], axis=1),
        "rope": rope_table(),
        "ident": np.eye(P, dtype=np.float32),
        "iota": np.arange(TOPK, dtype=np.float32)[None],
        "uv": np.concatenate([f["u_table"][0], f["v_table"][0]], axis=1),
    }
    arrays = {f"in_{k}": np.ascontiguousarray(a) for k, a in arrays.items()}
    nc = bacc.Bacc("TRN2", target_bir_lowering=False, num_devices=1)
    args = [nc.dram_tensor(k, a.shape, mybir.dt.from_np(a.dtype), kind="ExternalInput").ap() for k, a in arrays.items()]
    out = nc.dram_tensor("out", (T, D), F32, kind="ExternalOutput").ap()
    build(nc, *args, out)
    r = run_bass_kernel_spmd(nc, [arrays], core_ids=[0])
    return r.results[0]["out"].reshape(1, T, D)
```

```python
from contextlib import ExitStack

import numpy as np

import concourse.bass as bass
from concourse import mybir

F32 = mybir.dt.float32
U32 = mybir.dt.uint32
I32 = mybir.dt.int32
ALU = mybir.AluOpType
ACT = mybir.ActivationFunctionType
AX = mybir.AxisListType
ds = bass.ds

P = 128
T, D = 512, 1024
NB = T // P
KD = D // P
HD = 64
AH, BH = 8, 4
NS_A, NS_B = AH, 2 * BH
NSM = NS_A + NS_B
UNITS = AH + BH
KA, KB, VA, VB, QA, QB, GT, COLS = 0, 128, 640, 768, 1280, 1792, 2304, 4352
CW = 256
NCH = COLS // CW
KV_CH = QA // CW
QG_CH = NCH - KV_CH
WI_BUFS = 6
LATE = NB - 1
HEADS, NK, TOPK = 8, 128, 16
HI = 2 * HEADS
SLOTS = HEADS * TOPK
RING = 8
BATCH = 4
GROUPS = SLOTS // RING
BPG = RING // BATCH
ALPHA = 2.0 ** 0.25
LAMBDA_INIT = 0.8 - 0.6
EPS, LN_EPS = 1e-6, 1e-5
SCALE = HD ** -0.5
LOWEST = -3.0e38
N_W = 20

DVE_STEPS = 183
BEGIN_STEPS = 3
FIN_STEPS = 8

A_STEPS = UNITS + 3
ORDER = (["G", "gates", "rope", "G", "q_tiles", "G", "q_copy", "sigmoid"]
         + [x for u in range(A_STEPS) for x in ([f"attend{u}"] + (["G"] if u % 2 else []))]
         + ["subln", "G", "y_tiles", "y_copy", "G", "branches", "G", "merge", "G", "m_tiles", "m_copy", "outproj",
            "G", "G", "ln1", "G", "h_tiles", "h_copy", "query0", "G", "query1", "qq_copy0", "G", "query2", "qq_copy1",
            "G", "query3", "qq_copy2", "G", "qq_copy3", "key_scores", "G", "s_copy", "top0", "G", "top1", "G", "top2",
            "G", "top3", "cand", "G", "best0", "G", "best1", "G", "choose0", "G", "choose1"])
BATCHES = SLOTS // BATCH
assert ORDER.count("G") <= BATCHES
ORDER += ["G"] * (BATCHES - ORDER.count("G"))
LATE_GROUPS = QG_CH // 2


def build(nc, x_d, xT_d, win_d, wch_d, bgate_d, ln1_d, ln2_d, gains_d, subln_d, lam_d, rope_d, ident_d, iota_d,
          uv_d, out_d):
    with ExitStack() as ctx:
        def sb(name, shape, dt=F32):
            return ctx.enter_context(nc.sbuf_tensor(name, shape, dt))

        def sem(name):
            return ctx.enter_context(nc.semaphore(name))

        bank = [ctx.enter_context(nc.psum_tensor(f"bank{i}", [P, 512], F32)) for i in range(8)]

        ring = sb("ring", [P, RING * 2 * D])
        proj = sb("proj", [P, NB * COLS])
        kT = sb("kT", [P, 5 * T])
        wbuf = sb("wbuf", [P, 2, 2048])
        work = sb("work", [P, 6144])
        h_new = sb("h_new", [P, D])
        h_cur = sb("h_cur", [P, D])
        diag = sb("diag", [P, RING // 2, P])
        y_dve = sb("y_dve", [P, D])
        ident = sb("ident", [P, P])
        zeros = sb("zeros", [P, P])
        rope = sb("rope", [P, 4, NB * HD])
        gains = sb("gains", [P, 2, HD])
        subln = sb("subln", [P, 2 * HD])
        iota16 = sb("iota16", [P, TOPK])
        lam_e = sb("lam_e", [P, 4])
        neg_lam = sb("neg_lam", [P, 1])
        ss = sb("ss", [P, 8])
        root = sb("root", [P, 8])
        rinv = sb("rinv", [P, 8])
        negmax = sb("negmax", [P, NSM])
        rsum = sb("rsum", [P, NSM])
        rs_inv = sb("rs_inv", [P, NSM])
        stats = sb("stats", [P, 2, 6])
        mv = sb("mv", [P, 2])
        fstats = sb("fstats", [P, 2, 6])
        fmv = sb("fmv", [P, 2])
        froot = sb("froot", [P, 1])
        sv = sb("sv", [P, HI, TOPK])
        si = sb("si", [P, HI, TOPK], U32)
        cv = sb("cv", [P, HEADS, TOPK])
        ci = sb("ci", [P, HEADS, TOPK], U32)
        gsum = sb("gsum", [P, HEADS])
        idx_new = sb("idx_new", [P, SLOTS], I32)
        idx_cur = sb("idx_cur", [P, SLOTS], I32)
        idx_slot = sb("idx_slot", [P, RING], I32)
        gate_new = sb("gate_new", [P, SLOTS])
        gate_cur = sb("gate_cur", [P, SLOTS])
        dots = sb("dots", [P, RING])
        gelu = sb("gelu", [P, RING])
        wts = sb("wts", [P, RING])

        def uv(k):
            return ring[:, k * 2 * D:(k + 1) * 2 * D]

        xT = ring[:, 0:KD * T].rearrange("p (b k t) -> p b k t", b=NB, k=KD)
        wi_flat = [ring[:, KD * T + i * KD * CW:KD * T + (i + 1) * KD * CW] for i in range(WI_BUFS)]
        wi = [piece.rearrange("p (k c) -> p k c", k=KD) for piece in wi_flat]

        def W(i, n=1024):
            return work[:, i * 1024:i * 1024 + n]

        xT_late = W(0, LATE * D).rearrange("p (b k t) -> p b k t", b=LATE, k=KD)
        qrot, qT = W(0), W(1).rearrange("p (t q) -> p t q", t=8)
        yT, mT = W(0).rearrange("p (t q) -> p t q", t=8), W(1).rearrange("p (t q) -> p t q", t=8)
        probs = [work[:, 2048 + 512 * i:2560 + 512 * i] for i in range(4)]
        pT = [work[:, 4096 + 512 * i:4608 + 512 * i] for i in range(2)]
        yab = W(5)
        merged, xblk = W(2), W(3)
        hT = W(4).rearrange("p (t q) -> p t q", t=8)
        qqT = W(2, 2048).rearrange("p (t q) -> p t q", t=HI)
        s = W(0, 2048).rearrange("p (t n) -> p t n", t=HI)
        cand = W(2, 2048).rearrange("p (h n) -> p h n", h=HEADS)
        eq1 = W(4, 2048).rearrange("p (k a) -> p k a", a=TOPK)
        eq2 = W(0, 2048).rearrange("p (k a) -> p k a", a=TOPK)
        small = [work[:, 2048 + SLOTS * i:2048 + SLOTS * (i + 1)] for i in range(16)]
        ln2 = W(0, 2048)
        y_out = W(5)

        consts_landed = sem("consts_landed")
        zeros_set = sem("zeros_set")
        xT_landed = [sem(f"xT_landed{b}") for b in range(NB)]
        wi_landed = [sem(f"wi_landed{i}") for i in range(WI_BUFS)]
        tiles_ready = sem("tiles_ready")
        tiles_by_act = sem("tiles_by_act")
        tiles_by_dve = sem("tiles_by_dve")
        xT_late_landed = sem("xT_late_landed")
        late_landed = [sem("late_landed0"), sem("late_landed1")]
        late_tiles_ready = sem("late_tiles_ready")
        late_tiles_copied = sem("late_tiles_copied")
        key_meansq_ready = sem("key_meansq_ready")
        key_roots_ready = sem("key_roots_ready")
        keys_roped = sem("keys_roped")
        key_tiles_ready = sem("key_tiles_ready")
        kT_ready = sem("kT_ready")
        lam_dots_ready = sem("lam_dots_ready")
        lam_exp_ready = sem("lam_exp_ready")
        setup_step = sem("setup_step")
        w_landed = [sem("w_landed0"), sem("w_landed1")]
        x_landed = sem("x_landed")
        dve_step = sem("dve_step")
        meansq_ready = sem("meansq_ready")
        roots_ready = sem("roots_ready")
        gate_logits_ready = sem("gate_logits_ready")
        gates_ready = sem("gates_ready")
        q_roped = sem("q_roped")
        q_tiles_ready = sem("q_tiles_ready")
        qT_ready = sem("qT_ready")
        scores_ready = sem("scores_ready")
        negmax_ready = sem("negmax_ready")
        probs_ready = sem("probs_ready")
        combined_ready = sem("combined_ready")
        pT_tiles_ready = sem("pT_tiles_ready")
        pT_ready = sem("pT_ready")
        o_ready = sem("o_ready")
        o_taken = sem("o_taken")
        y_ready = sem("y_ready")
        y_tiles_ready = sem("y_tiles_ready")
        yT_ready = sem("yT_ready")
        branch_ready = sem("branch_ready")
        merged_ready = sem("merged_ready")
        m_tiles_ready = sem("m_tiles_ready")
        mT_ready = sem("mT_ready")
        outproj_ready = sem("outproj_ready")
        h_ready = sem("h_ready")
        h_tiles_ready = sem("h_tiles_ready")
        hT_ready = sem("hT_ready")
        query_ready = sem("query_ready")
        qqT_ready = sem("qqT_ready")
        keyscores_ready = sem("keyscores_ready")
        s_ready = sem("s_ready")
        cv_shifted = sem("cv_shifted")
        gate_exp_ready = sem("gate_exp_ready")
        chosen = sem("chosen")
        idx_taken = sem("idx_taken")
        idx_staged = sem("idx_staged")
        pe_slots_free = sem("pe_slots_free")
        dve_slots_free = sem("dve_slots_free")
        gather_step = sem("gather_step")
        waits_passed = sem("waits_passed")
        uv_landed = [sem(f"uv_landed{k}") for k in range(RING)]
        dots_ready = sem("dots_ready")
        gelu_ready = sem("gelu_ready")
        diag_ready = sem("diag_ready")
        y_free = sem("y_free")
        var_ready = sem("var_ready")
        froot_ready = sem("froot_ready")
        fin_step = sem("fin_step")
        begin_step = sem("begin_step")
        out_ready = sem("out_ready")
        out_stored = sem("out_stored")
        ln2_landed = sem("ln2_landed")

        N_CONSTS = 6
        block = ctx.enter_context(nc.Block())

        def softmaxes(u):
            return [u] if u < AH else [AH + 2 * (u - AH), AH + 2 * (u - AH) + 1]

        class Steps:
            def __init__(self, eng, semaphore, base):
                self.eng, self.sem, self.base, self.n = eng, semaphore, base, 0

            def did(self, ins):
                ins.then_inc(self.sem, 1)
                self.n += 1

            def wait(self):
                self.eng.wait_ge(self.sem, self.base + self.n)

            def pass_wait(self):
                self.wait()
                self.eng.sem_inc(waits_passed, 1)

            def alone(self, ins):
                self.did(ins)
                self.wait()

        def in_order(stage, batch, b, done=0):
            n = place = 0
            for name in ORDER:
                if name != "G":
                    stage(name, b)
                elif batch is not None:
                    place += 1
                    if place * (BATCHES - done) // BATCHES > n:
                        batch(b - 1, (done + n) // BPG, (done + n) % BPG)
                        n += 1

        @block.sync
        def _(sp):
            def load_piece(p):
                sp.dma_start(wi_flat[p % WI_BUFS], win_d[p * P:(p + 1) * P, :]).then_inc(wi_landed[p % WI_BUFS], 16)

            for tb in range(NB):
                sp.dma_start(ring[:, tb * D:(tb + 1) * D], xT_d[tb]).then_inc(xT_landed[tb], 16)
                if tb == 0:
                    load_piece(0)
            for p in range(1, 3):
                load_piece(p)
            sp.dma_start(ident[:], ident_d).then_inc(consts_landed, 16)
            sp.dma_start(rope[:], rope_d).then_inc(consts_landed, 16)
            sp.dma_start(gains[:].rearrange("p a d -> p (a d)"), gains_d.to_broadcast([P, 2 * HD])).then_inc(consts_landed, 16)
            sp.dma_start(subln[:], subln_d.to_broadcast([P, 2 * HD])).then_inc(consts_landed, 16)
            sp.dma_start(iota16[:], iota_d.to_broadcast([P, TOPK])).then_inc(consts_landed, 16)
            sp.dma_start(W(5, 4 * HD), lam_d.to_broadcast([P, 4 * HD])).then_inc(consts_landed, 16)
            for p in range(3, NCH):
                if p >= WI_BUFS:
                    q = p - WI_BUFS
                    sp.wait_ge(tiles_ready, (q + 1) * NB if q < KV_CH else KV_CH * NB + q - KV_CH + 1)
                load_piece(p)

            release = ([(gate_logits_ready, 2, 1), (gate_logits_ready, 2, 2)]
                       + [(branch_ready, 4, n + 1) for n in range(4)]
                       + [(outproj_ready, 4, n + 1) for n in range(4)]
                       + [(h_ready, 1, 1)]
                       + [(query_ready, 8, n + 1) for n in range(8)]
                       + [(keyscores_ready, 4, 4)])
            assert len(release) == N_W

            def stream(b, before):
                for n in range(N_W):
                    if n == 4:
                        sp.wait_ge(y_tiles_ready, 2 * b + 1)
                        sp.dma_start(xblk, x_d[ds(b * P, P), :]).then_inc(x_landed, 16)
                    if n >= 2:
                        semaphore, per_block, count = release[n - 2]
                        sp.wait_ge(semaphore, b * per_block + count)
                    elif before is not None:
                        sp.wait_ge(*before[n])
                    buf = wbuf[:, n % 2, :]
                    landed = w_landed[n % 2]
                    if n < 2:
                        sp.dma_start(buf[:, 0:D], bgate_d[:, n * D:(n + 1) * D].to_broadcast([P, D])).then_inc(landed, 16)
                    elif n == 10:
                        sp.dma_start(buf, ln1_d.to_broadcast([P, 2 * D])).then_inc(landed, 16)
                    else:
                        sp.dma_start(buf, wch_d[n - 2 - (n > 10)]).then_inc(landed, 16)

            def store(c):
                sp.wait_ge(out_ready, c + 1)
                sp.dma_start(out_d[ds(c * P, P), :], y_out).then_inc(out_stored, 16)

            sp.sem_inc(out_stored, 16)
            stream(0, None)
            sp.wait_ge(chosen, 1)
            sp.dma_start(W(0, LATE * D).rearrange("p (b c) -> p b c", b=LATE),
                         xT_d[1:NB].rearrange("b p c -> p b c")).then_inc(xT_late_landed, 16)
            for j in range(2):
                sp.wait_ge(keyscores_ready if j else query_ready, 4 if j else 8)
                sp.dma_start(wbuf[:, j, :], win_d[(KV_CH + j) * P:(KV_CH + j + 1) * P, :]).then_inc(late_landed[j], 16)
            with sp.Fori(1, LATE_GROUPS) as it:
                for j in range(2):
                    sp.wait_ge(late_tiles_ready, (it * 2 + j - 1) * LATE)
                    sp.dma_start(wbuf[:, j, :], win_d[ds((it * 2 + KV_CH + j) * P, P), :]).then_inc(late_landed[j], 16)

            def round_(b, before):
                stream(b, before)
                sp.wait_ge(chosen, b + 1)
                sp.dma_start(ln2, ln2_d.to_broadcast([P, 2 * D])).then_inc(ln2_landed, 16)
                store(b - 1)

            round_(1, [(late_tiles_ready, (QG_CH - 1) * LATE), (late_tiles_ready, QG_CH * LATE)])
            with sp.Fori(2, NB) as b:
                round_(b, [(query_ready, b * 8), (keyscores_ready, b * 4)])
            store(NB - 1)
            sp.wait_ge(out_stored, 16 * (NB + 1))

        @block.gpsimd
        def _(pool):
            nc.gpsimd.memset(zeros[:], 0.0).then_inc(zeros_set, 1)
            pool.wait_ge(tiles_ready, KV_CH * NB + QG_CH)

            def begin(c):
                pool.wait_ge(chosen, c + 1)
                pool.sem_inc(waits_passed, 1)
                nc.gpsimd.tensor_copy(idx_cur[:], idx_new[:]).then_inc(idx_taken, 1)
                pool.wait_ge(idx_taken, c + 1)
                pool.sem_inc(waits_passed, 1)

            def group(G, g):
                for k in range(RING):
                    pool.wait_ge(dve_slots_free if k % 2 else pe_slots_free, G * (RING // 2) + k // 2 + 1)
                    if k % BATCH == 0:
                        nc.gpsimd.tensor_copy(idx_slot[:, k:k + BATCH],
                                              idx_cur[:, ds(g * RING + k, BATCH)]).then_inc(idx_staged, 1)
                        pool.wait_ge(idx_staged, G * (RING // BATCH) + k // BATCH + 1)
                    pool.sem_inc(waits_passed, 1)
                    nc.gpsimd.indirect_dma_start(
                        out=uv(k), out_offset=None, in_=uv_d,
                        in_offset=bass.IndirectOffsetOnAxis(ap=idx_slot[:, k:k + 1], axis=0)).then_inc(uv_landed[k], 16)

            with pool.Fori(0, NB) as c:
                begin(c)
                with pool.Fori(0, GROUPS) as g:
                    group(c * GROUPS + g, g)

        @block.vector
        def _(dve):
            v = nc.vector
            dve.sem_inc(tiles_by_dve, 4)
            dve.sem_inc(y_free, 1)
            dve.sem_inc(dve_slots_free, RING // 2)
            for p in range(KV_CH):
                for tb in (2, 3):
                    dve.wait_ge(tiles_ready, p * NB + tb + 1)
                    v.tensor_copy(proj[:, tb * COLS + p * CW:tb * COLS + (p + 1) * CW],
                                  bank[p % 2 * 4 + tb][:, 0:CW]).then_inc(tiles_by_dve, 1)

            setup = Steps(dve, setup_step, 0)

            def rope_tables(kind, b):
                return rope[:, 2 * kind, ds(b * HD, HD)], rope[:, 2 * kind + 1, ds(b * HD, HD)]

            def rotate(steps, out, x, tmp, n, kind, b, last):
                cos, sin = rope_tables(kind, b)
                parts = 2 if kind == 0 else 1
                half = HD // parts // 2
                m = n * parts
                hv = "p (m s d) -> p m s d"
                x4 = x.rearrange(hv, m=m, s=2)
                t4 = tmp.rearrange(hv, m=m, s=2)
                s4 = sin.rearrange("p (a s d) -> p a s d", a=parts, s=2)
                for side in range(2):
                    if kind == 0:
                        o_ap = t4[:, :, side, :].rearrange("p (n a) d -> p n a d", a=2)
                        x_ap = x4[:, :, 1 - side, :].rearrange("p (n a) d -> p n a d", a=2)
                        s_ap = s4[:, :, side, :].unsqueeze(1).to_broadcast([P, n, 2, half])
                    else:
                        o_ap, x_ap = t4[:, :, side, :], x4[:, :, 1 - side, :]
                        s_ap = s4[:, 0, side, :].unsqueeze(1).to_broadcast([P, n, half])
                    steps.did(v.tensor_tensor(o_ap, x_ap, s_ap, ALU.mult))
                hx = "p (n d) -> p n d"
                steps.alone(v.tensor_tensor(out.rearrange(hx, n=n), x.rearrange(hx, n=n),
                                            cos.unsqueeze(1).to_broadcast([P, n, HD]), ALU.mult))
                ins = v.tensor_tensor(out, out, tmp, ALU.add)
                if last is None:
                    steps.did(ins)
                else:
                    ins.then_inc(last, 1)

            dve.wait_ge(tiles_by_act, 4 + 2 * KV_CH)
            dve.wait_ge(tiles_by_dve, 4 + 2 * KV_CH)
            dve.wait_ge(consts_landed, 16 * N_CONSTS)
            krot = work[:, 0:2560]
            sq, ktmp, ky = work[:, 2560:3072], work[:, 3072:3584], work[:, 3584:4096]
            ka = proj[:].rearrange("p (b c) -> p b c", b=NB)[:, :, KA:KA + 2 * HD]
            setup.alone(v.tensor_tensor(sq.rearrange("p (b c) -> p b c", b=NB), ka, ka, ALU.mult))
            setup.alone(v.tensor_reduce(ss[:], sq.rearrange("p (n d) -> p n d", d=HD), AX.X, ALU.add))
            v.tensor_scalar(ss[:], ss[:], 1.0 / HD, EPS, ALU.mult, ALU.add).then_inc(key_meansq_ready, 1)
            lam = W(5, 4 * HD).rearrange("p (a d) -> p a d", a=4)
            lam_prod = work[:, 5120 + 4 * HD:5120 + 6 * HD].rearrange("p (a d) -> p a d", a=2)
            for a in range(2):
                setup.did(v.tensor_tensor(lam_prod[:, a, :], lam[:, 2 * a, :], lam[:, 2 * a + 1, :], ALU.mult))
            setup.wait()
            v.tensor_reduce(lam_e[:, 0:2], lam_prod, AX.X, ALU.add).then_inc(lam_dots_ready, 1)
            setup.did(v.tensor_scalar(subln[:], subln[:], 1.0 - LAMBDA_INIT, None, ALU.mult))
            dve.wait_ge(lam_exp_ready, 1)
            setup.alone(v.tensor_tensor(neg_lam[:], lam_e[:, 3:4], lam_e[:, 2:3], ALU.subtract))
            setup.alone(v.tensor_scalar(neg_lam[:], neg_lam[:], -LAMBDA_INIT, None, ALU.add))
            dve.wait_ge(key_roots_ready, 1)
            setup.alone(v.reciprocal(rinv[:], root[:]))
            for kb in range(NB):
                base = kb * COLS
                k3 = proj[:, base + KA:base + KA + 2 * HD].rearrange("p (n d) -> p n d", n=2)
                y3 = ky[:, 0:2 * HD].rearrange("p (n d) -> p n d", n=2)
                setup.alone(v.tensor_tensor(y3, k3, rinv[:, 2 * kb:2 * kb + 2].unsqueeze(2).to_broadcast([P, 2, HD]),
                                            ALU.mult))
                setup.alone(v.tensor_tensor(y3, y3, gains[:, 1, :].unsqueeze(1).to_broadcast([P, 2, HD]), ALU.mult))
                out = krot[:, kb * 640:(kb + 1) * 640]
                rotate(setup, out[:, 0:128], ky[:, 0:128], ktmp[:, 0:128], 2, 0, kb, None)
                setup.wait()
                rotate(setup, out[:, 128:640], proj[:, base + KB:base + KB + 512], ktmp, 8, 1, kb, keys_roped)
                setup.wait()

            def root_of(steps, b, which, src, n, scale, eps):
                v.tensor_scalar(ss[:, 0:n], src, scale, eps, ALU.mult, ALU.add).then_inc(meansq_ready, 1)
                dve.wait_ge(roots_ready, 3 * b + which + 1)
                steps.alone(v.reciprocal(rinv[:, 0:n], root[:, 0:n]))

            hold = {}

            def landed(b, n):
                dve.wait_ge(w_landed[n % 2], 16 * (b * (N_W // 2) + n // 2 + 1))

            def top16(steps, vals, best, index, rows):
                for j in rows:
                    steps.did(v.max(best(j)[:, 0:8], vals(j)))
                steps.pass_wait()
                for j in rows:
                    steps.did(v.max_index(index(j)[:, 0:8], best(j)[:, 0:8], vals(j)))
                for j in rows:
                    steps.did(v.match_replace(vals(j), best(j)[:, 0:8], vals(j), LOWEST))
                steps.pass_wait()
                for j in rows:
                    steps.did(v.max(best(j)[:, 8:16], vals(j)))
                steps.pass_wait()
                for j in rows:
                    steps.did(v.max_index(index(j)[:, 8:16], best(j)[:, 8:16], vals(j)))

            def attend(b, step):
                steps = hold["steps"]
                if step < UNITS:
                    for m in softmaxes(step):
                        dve.wait_ge(scores_ready, b * NSM + m + 1)
                        v.tensor_reduce(negmax[:, m:m + 1], bank[2 + m % 2][:], AX.X, ALU.max,
                                        negate=True).then_inc(negmax_ready, 1)
                u = step - 1
                if AH <= u < UNITS:
                    m0, m1 = softmaxes(u)
                    dve.wait_ge(probs_ready, b * NSM + m1 + 1)
                    steps.alone(v.reciprocal(rs_inv[:, m0:m1 + 1], rsum[:, m0:m1 + 1]))
                    steps.did(v.tensor_scalar(probs[m0 % 4], probs[m0 % 4], rs_inv[:, m0:m0 + 1], None, ALU.mult))
                    steps.alone(v.tensor_scalar(rs_inv[:, m1:m1 + 1], rs_inv[:, m1:m1 + 1],
                                                neg_lam[:, 0:1], None, ALU.mult))
                    v.scalar_tensor_tensor(probs[m0 % 4], probs[m1 % 4], rs_inv[:, m1:m1 + 1], probs[m0 % 4],
                                           ALU.mult, ALU.add).then_inc(combined_ready, 1)
                u = step - 3
                if 0 <= u < AH:
                    dve.wait_ge(probs_ready, b * NSM + u + 1)
                    steps.alone(v.reciprocal(rs_inv[:, u:u + 1], rsum[:, u:u + 1]))
                    dve.wait_ge(o_ready, b * UNITS + u + 1)
                    v.tensor_scalar(yab[:, u * HD:(u + 1) * HD], bank[6 + u % 2][:, 0:HD],
                                    rs_inv[:, u:u + 1], None, ALU.mult).then_inc(o_taken, 1)
                elif AH <= u < UNITS:
                    dve.wait_ge(o_ready, b * UNITS + u + 1)
                    c0 = AH * HD + (u - AH) * 2 * HD
                    v.tensor_copy(yab[:, c0:c0 + 2 * HD], bank[6 + u % 2][:, 0:2 * HD]).then_inc(o_taken, 1)

            def stages(name, b):
                if name == "gates":
                    hold["steps"] = Steps(dve, dve_step, b * DVE_STEPS)
                steps = hold["steps"]
                if name == "gates":
                    if isinstance(b, int):
                        dve.wait_ge(late_tiles_copied if b else tiles_by_act,
                                    (QG_CH + 2) * LATE if b else 4 + 2 * KV_CH + QG_CH)
                    for n in range(2):
                        landed(b, n)
                        g = proj[:, ds(b * COLS + GT + n * D, D)]
                        v.tensor_tensor(g, g, wbuf[:, n, 0:D], ALU.add).then_inc(gate_logits_ready, 1)
                elif name == "rope":
                    if isinstance(b, int) and b == 0:
                        dve.wait_ge(keys_roped, NB)
                        dve.wait_ge(key_tiles_ready, 5)
                    else:
                        dve.wait_ge(out_stored, b * 16)
                    q = proj[:, ds(b * COLS + QA, 512)]
                    sq, qy, tmp = W(2, 512), W(3, 512), W(4, 512)
                    hx = "p (n d) -> p n d"
                    steps.alone(v.tensor_tensor(sq, q, q, ALU.mult))
                    steps.alone(v.tensor_reduce(ss[:], sq.rearrange(hx, n=AH), AX.X, ALU.add))
                    root_of(steps, b, 0, ss[:], AH, 1.0 / HD, EPS)
                    steps.alone(v.tensor_tensor(qy.rearrange(hx, n=AH), q.rearrange(hx, n=AH),
                                                rinv[:].unsqueeze(2).to_broadcast([P, AH, HD]), ALU.mult))
                    steps.alone(v.tensor_tensor(qy.rearrange(hx, n=AH), qy.rearrange(hx, n=AH),
                                                gains[:, 0, :].unsqueeze(1).to_broadcast([P, AH, HD]), ALU.mult))
                    rotate(steps, qrot[:, 0:512], qy, tmp, AH, 0, b, q_roped)
                    rotate(steps, qrot[:, 512:1024], proj[:, ds(b * COLS + QB, 512)], W(5, 512), NS_B, 1, b, q_roped)
                elif name.startswith("attend"):
                    attend(b, int(name[6:]))
                elif name == "subln":
                    dve.wait_ge(o_taken, (b + 1) * UNITS)
                    yb = yab[:, 512:1024]
                    sq = W(3, 512)
                    hx = "p (n d) -> p n d"
                    steps.alone(v.tensor_tensor(sq, yb, yb, ALU.mult))
                    steps.alone(v.tensor_reduce(ss[:, 0:BH], sq.rearrange(hx, n=BH), AX.X, ALU.add))
                    root_of(steps, b, 1, ss[:, 0:BH], BH, 1.0 / (2 * HD), EPS)
                    steps.alone(v.tensor_tensor(yb.rearrange(hx, n=BH), yb.rearrange(hx, n=BH),
                                                rinv[:, 0:BH].unsqueeze(2).to_broadcast([P, BH, 2 * HD]), ALU.mult))
                    v.tensor_tensor(yb.rearrange(hx, n=BH), yb.rearrange(hx, n=BH),
                                    subln[:].unsqueeze(1).to_broadcast([P, BH, 2 * HD]), ALU.mult).then_inc(y_ready, 1)
                elif name == "merge":
                    dve.wait_ge(gates_ready, 2 * b + 2)
                    for n in range(2):
                        gA = proj[:, ds(b * COLS + GT + n * 512, 512)]
                        gB = proj[:, ds(b * COLS + GT + D + n * 512, 512)]
                        m, t = merged[:, n * 512:(n + 1) * 512], yab[:, n * 512:(n + 1) * 512]
                        dve.wait_ge(branch_ready, 4 * b + 2 * n + 1)
                        steps.did(v.tensor_tensor(m, gA, bank[4 + 2 * n][:], ALU.mult))
                        dve.wait_ge(branch_ready, 4 * b + 2 * n + 2)
                        steps.alone(v.tensor_tensor(t, gB, bank[5 + 2 * n][:], ALU.mult))
                        v.tensor_tensor(m, m, t, ALU.add).then_inc(merged_ready, 1)
                elif name == "ln1":
                    dve.wait_ge(x_landed, 16 * (b + 1))
                    for n in range(2):
                        c = slice(n * 512, (n + 1) * 512)
                        dve.wait_ge(outproj_ready, 4 * b + 2 * n + 2)
                        steps.alone(v.scalar_tensor_tensor(h_new[:, c], xblk[:, c], ALPHA, bank[4 + n][:],
                                                           ALU.mult, ALU.add))
                        steps.did(v.bn_stats(stats[:, n, :], h_new[:, c]))
                    steps.pass_wait()
                    steps.alone(v.bn_aggr(mv[:], stats[:]))
                    root_of(steps, b, 2, mv[:, 1:2], 1, 1.0, LN_EPS)
                    steps.alone(v.tensor_scalar(h_new[:], h_new[:], mv[:, 0:1], rinv[:, 0:1], ALU.subtract, ALU.mult))
                    landed(b, 10)
                    steps.alone(v.tensor_tensor(h_new[:], h_new[:], wbuf[:, 0, 0:D], ALU.mult))
                    v.tensor_tensor(h_new[:], h_new[:], wbuf[:, 0, D:2 * D], ALU.add).then_inc(h_ready, 1)
                elif name.startswith("top"):
                    n = int(name[-1])
                    dve.wait_ge(s_ready, 4 * b + n + 1)
                    dve.sem_inc(waits_passed, 1)
                    top16(steps, lambda j: s[:, j, :], lambda j: sv[:, j, :], lambda j: si[:, j, :],
                          range(4 * n, 4 * n + 4))
                elif name == "cand":
                    steps.wait()
                    sv4 = sv[:].rearrange("p (h i) k -> p h i k", i=2)
                    steps.alone(v.tensor_tensor(
                        cand.rearrange("p h (a b) -> p h a b", a=TOPK),
                        sv4[:, :, 0, :].unsqueeze(3).to_broadcast([P, HEADS, TOPK, TOPK]),
                        sv4[:, :, 1, :].unsqueeze(2).to_broadcast([P, HEADS, TOPK, TOPK]), ALU.add))
                elif name in ("best0", "best1"):
                    steps.pass_wait()
                    n = int(name[-1])
                    top16(steps, lambda j: cand[:, j, :], lambda j: cv[:, j, :], lambda j: ci[:, j, :],
                          range(4 * n, 4 * n + 4))
                elif name == "choose0":
                    steps.wait()
                    steps.alone(v.tensor_copy(gsum[:], cv[:, :, 0]))
                    v.tensor_tensor(cv[:], cv[:], gsum[:].unsqueeze(2).to_broadcast([P, HEADS, TOPK]),
                                    ALU.subtract).then_inc(cv_shifted, 1)
                    cif = ci[:].rearrange("p h k -> p (h k)")
                    pa, pb = small[0].bitcast(U32), small[1].bitcast(U32)
                    paf, pbf = small[2], small[3]
                    sif = work[:, 2048 + 8 * SLOTS:2048 + 10 * SLOTS].rearrange("p (h i k) -> p h i k", h=HEADS, i=2)
                    steps.did(v.tensor_scalar(pa, cif, 4, None, ALU.logical_shift_right))
                    steps.did(v.tensor_scalar(pb, cif, TOPK - 1, None, ALU.bitwise_and))
                    steps.alone(v.tensor_copy(sif, si[:].rearrange("p (h i) k -> p h i k", i=2)))
                    steps.did(v.tensor_copy(paf, pa))
                    steps.alone(v.tensor_copy(pbf, pb))
                elif name == "choose1":
                    paf, pbf, e1, e2 = small[2], small[3], small[4], small[5]
                    sif = work[:, 2048 + 8 * SLOTS:2048 + 10 * SLOTS].rearrange("p (h i k) -> p h i k", h=HEADS, i=2)
                    for pf, eq, e, i in ((paf, eq1, e1, 0), (pbf, eq2, e2, 1)):
                        steps.alone(v.tensor_tensor(eq, pf.unsqueeze(2).to_broadcast([P, SLOTS, TOPK]),
                                                    iota16[:].unsqueeze(1).to_broadcast([P, SLOTS, TOPK]), ALU.is_equal))
                        eq4 = eq.rearrange("p (h k) a -> p h k a", h=HEADS)
                        steps.alone(v.tensor_tensor(eq4, eq4, sif[:, :, i, :].unsqueeze(2)
                                                    .to_broadcast([P, HEADS, TOPK, TOPK]), ALU.mult))
                        steps.alone(v.tensor_reduce(e, eq, AX.X, ALU.add))
                    dve.wait_ge(gate_exp_ready, b + 1)
                    steps.alone(v.tensor_reduce(gsum[:], cv[:], AX.X, ALU.add))
                    steps.alone(v.reciprocal(gsum[:], gsum[:]))
                    steps.did(v.tensor_tensor(gate_new[:].rearrange("p (h k) -> p h k", h=HEADS), cv[:],
                                              gsum[:].unsqueeze(2).to_broadcast([P, HEADS, TOPK]), ALU.mult))
                    if not isinstance(b, int) or b > 0:
                        dve.wait_ge(idx_taken, b)
                    v.scalar_tensor_tensor(idx_new[:], e1, float(NK), e2, ALU.mult, ALU.add).then_inc(chosen, 1)
                    assert steps.n == DVE_STEPS, steps.n

            def batch(c, g, bt):
                G = c * GROUPS + g
                B = G * BPG + bt
                ks = range(bt * BATCH, (bt + 1) * BATCH)
                for k in ks:
                    dve.wait_ge(uv_landed[k], (G + 1) * 16)
                    u = uv(k)[:, 0:D]
                    ins = v.tensor_tensor_reduce(out=u, in0=u, in1=h_cur[:], scale=1.0, scalar=0.0, op0=ALU.mult,
                                                 op1=ALU.add, accum_out=dots[:, k:k + 1])
                ins.then_inc(dots_ready, 1)
                steps = Steps(dve, gather_step, B)
                dve.wait_ge(gelu_ready, B + 1)
                sl = slice(bt * BATCH, (bt + 1) * BATCH)
                steps.alone(v.tensor_tensor(wts[:, sl], gelu[:, sl], gate_cur[:, ds(g * RING + bt * BATCH, BATCH)],
                                            ALU.mult))
                dve.wait_ge(pe_slots_free, G * (RING // 2) + (bt + 1) * (BATCH // 2))
                for k in ks[::2]:
                    v.tensor_scalar(diag[:, k // 2, :], ident[:], wts[:, k:k + 1], None, ALU.mult).then_inc(diag_ready, 1)
                for k in ks[1::2]:
                    v.scalar_tensor_tensor(y_dve[:], uv(k)[:, D:2 * D], wts[:, k:k + 1], y_dve[:],
                                           ALU.mult, ALU.add).then_inc(dve_slots_free, 1)
                    dve.wait_ge(dve_slots_free, (G + 1) * (RING // 2) + k // 2 + 1)

            def begin(b):
                steps = Steps(dve, begin_step, b * BEGIN_STEPS)
                dve.wait_ge(dve_step, (b + 1) * DVE_STEPS)
                steps.did(v.memset(y_dve[:], 0.0))
                steps.did(v.tensor_copy(gate_cur[:], gate_new[:]))
                steps.alone(v.tensor_copy(h_cur[:], h_new[:]))
                assert steps.n == BEGIN_STEPS, steps.n

            def add_up(c):
                steps = Steps(dve, fin_step, c * FIN_STEPS)
                dve.wait_ge(pe_slots_free, (c + 1) * (SLOTS // 2) + RING // 2)
                for n in range(2):
                    col = slice(n * 512, (n + 1) * 512)
                    steps.did(v.scalar_tensor_tensor(y_out[:, col], h_cur[:, col], ALPHA, bank[n][:], ALU.mult, ALU.add))
                steps.wait()
                v.tensor_tensor(y_out, y_out, y_dve[:], ALU.add).then_inc(y_free, 1)
                dve.wait_ge(y_free, c + 2)
                return steps

            def finish(c, steps):
                for n in range(2):
                    steps.did(v.bn_stats(fstats[:, n, :], y_out[:, n * 512:(n + 1) * 512]))
                steps.pass_wait()
                steps.alone(v.bn_aggr(fmv[:], fstats[:]))
                v.tensor_scalar(fmv[:, 1:2], fmv[:, 1:2], LN_EPS, None, ALU.add).then_inc(var_ready, 1)
                dve.wait_ge(froot_ready, c + 1)
                steps.alone(v.reciprocal(froot[:], froot[:]))
                steps.alone(v.tensor_scalar(y_out, y_out, fmv[:, 0:1], froot[:, 0:1], ALU.subtract, ALU.mult))
                dve.wait_ge(ln2_landed, 16 * (NB - 1) if isinstance(c, int) and c == NB - 1 else (c + 1) * 16)
                steps.alone(v.tensor_tensor(y_out, y_out, ln2[:, 0:D], ALU.mult))
                v.tensor_tensor(y_out, y_out, ln2[:, D:2 * D], ALU.add).then_inc(out_ready, 1)
                assert steps.n == FIN_STEPS, steps.n

            in_order(stages, None, 0)
            begin(0)

            def round_(b, done):
                in_order(stages, batch, b, done)
                steps = add_up(b - 1)
                begin(b)
                finish(b - 1, steps)

            with dve.Fori(0, LATE_GROUPS) as g:
                for bt in range(BPG):
                    batch(0, g, bt)
            round_(1, LATE_GROUPS * BPG)
            with dve.Fori(2, NB) as b:
                round_(b, 0)
            with dve.Fori(0, GROUPS) as g:
                for bt in range(BPG):
                    batch(NB - 1, g, bt)
            dve.wait_ge(out_stored, 16 * NB)
            finish(NB - 1, add_up(NB - 1))

        @block.scalar
        def _(act):
            a = nc.scalar
            act.sem_inc(tiles_by_act, 4)
            act.sem_inc(late_tiles_copied, 2 * LATE)
            for p in range(KV_CH):
                for tb in (0, 1):
                    act.wait_ge(tiles_ready, p * NB + tb + 1)
                    a.activation(proj[:, tb * COLS + p * CW:tb * COLS + (p + 1) * CW],
                                 bank[p % 2 * 4 + tb][:, 0:CW], ACT.Copy).then_inc(tiles_by_act, 1)

            def copy_first_block(n):
                act.wait_ge(tiles_ready, KV_CH * NB + n + 1)
                a.activation(proj[:, QA + n * CW:QA + (n + 1) * CW], bank[n % 2][:, 0:CW],
                             ACT.Copy).then_inc(tiles_by_act, 1)

            for n in range(2):
                copy_first_block(n)
            act.wait_ge(lam_dots_ready, 1)
            a.activation(lam_e[:, 2:4], lam_e[:, 0:2], ACT.Exp).then_inc(lam_exp_ready, 1)
            act.wait_ge(key_meansq_ready, 1)
            a.activation(root[:], ss[:], ACT.Sqrt).then_inc(key_roots_ready, 1)
            for n in range(2, QG_CH):
                copy_first_block(n)
            for t in range(5):
                act.wait_ge(key_tiles_ready, t + 1)
                a.activation(kT[:, t * T:(t + 1) * T], bank[2 + t][:], ACT.Copy).then_inc(kT_ready, 1)

            def take_root(b, which, n):
                act.wait_ge(meansq_ready, 3 * b + which + 1)
                a.activation(root[:, 0:n], ss[:, 0:n], ACT.Sqrt).then_inc(roots_ready, 1)

            def two_tiles(b, asked, done, dst, scale=1.0):
                for n in range(2):
                    act.wait_ge(asked, 2 * b + n + 1)
                    a.activation(dst[:, 4 * n:4 * n + 4, :].rearrange("p t q -> p (t q)"), bank[2 + n][:],
                                 ACT.Copy, scale=scale).then_inc(done, 1)

            def attend(b, step):
                u = step - 2
                if 0 <= u < UNITS:
                    act.wait_ge(pT_tiles_ready, b * UNITS + u + 1)
                    a.activation(pT[u % 2], bank[4 + u % 2][:], ACT.Copy).then_inc(pT_ready, 1)
                if step < UNITS:
                    for m in softmaxes(step):
                        act.wait_ge(negmax_ready, b * NSM + m + 1)
                        a.activation(probs[m % 4], bank[2 + m % 2][:], ACT.Exp, bias=negmax[:, m:m + 1],
                                     accum_out=rsum[:, m:m + 1]).then_inc(probs_ready, 1)

            def stages(name, b):
                if name == "sigmoid":
                    for n in range(2):
                        act.wait_ge(gate_logits_ready, 2 * b + n + 1)
                        g = proj[:, ds(b * COLS + GT + n * D, D)]
                        a.activation(g, g, ACT.Sigmoid).then_inc(gates_ready, 1)
                elif name == "rope":
                    take_root(b, 0, AH)
                elif name == "q_copy":
                    two_tiles(b, q_tiles_ready, qT_ready, qT, SCALE)
                elif name.startswith("attend"):
                    attend(b, int(name[6:]))
                elif name == "subln":
                    take_root(b, 1, BH)
                elif name == "y_copy":
                    two_tiles(b, y_tiles_ready, yT_ready, yT)
                elif name == "m_copy":
                    two_tiles(b, m_tiles_ready, mT_ready, mT)
                elif name == "ln1":
                    take_root(b, 2, 1)
                elif name == "h_copy":
                    two_tiles(b, h_tiles_ready, hT_ready, hT)
                elif name.startswith("qq_copy"):
                    n = int(name[-1])
                    act.wait_ge(query_ready, 8 * b + 2 * n + 2)
                    a.activation(qqT[:, 4 * n:4 * n + 4, :].rearrange("p t q -> p (t q)"), bank[4 + n][:],
                                 ACT.Copy).then_inc(qqT_ready, 1)
                elif name == "s_copy":
                    for n in range(4):
                        act.wait_ge(keyscores_ready, 4 * b + n + 1)
                        a.activation(s[:, 4 * n:4 * n + 4, :].rearrange("p t q -> p (t q)"), bank[2 + n][:],
                                     ACT.Copy).then_inc(s_ready, 1)
                elif name == "choose1":
                    act.wait_ge(cv_shifted, b + 1)
                    a.activation(cv[:], cv[:], ACT.Exp).then_inc(gate_exp_ready, 1)

            def batch(c, g, bt):
                act.wait_ge(dots_ready, (c * GROUPS + g) * BPG + bt + 1)
                a.activation(gelu[:, bt * BATCH:(bt + 1) * BATCH], dots[:, bt * BATCH:(bt + 1) * BATCH],
                             ACT.Gelu).then_inc(gelu_ready, 1)

            def finish(c):
                act.wait_ge(var_ready, c + 1)
                a.activation(froot[:], fmv[:, 1:2], ACT.Sqrt).then_inc(froot_ready, 1)

            in_order(stages, None, 0)

            with act.Fori(0, LATE_GROUPS) as g:
                for j in range(2):
                    for tb in range(1, NB):
                        act.wait_ge(late_tiles_ready, (g * 2 + j) * LATE + tb)
                        a.activation(proj[:, ds(tb * COLS + QA + (g * 2 + j) * CW, CW)],
                                     bank[1 + 3 * j + tb][:, 0:CW], ACT.Copy).then_inc(late_tiles_copied, 1)
                    batch(0, g, j)
            in_order(stages, batch, 1, LATE_GROUPS * BPG)
            finish(0)
            with act.Fori(2, NB) as b:
                in_order(stages, batch, b)
                finish(b - 1)
            with act.Fori(0, GROUPS) as g:
                for bt in range(BPG):
                    batch(NB - 1, g, bt)
            finish(NB - 1)

        @block.tensor
        def _(pe):
            t_ = nc.tensor
            pe.sem_inc(pe_slots_free, RING // 2)
            for p in range(KV_CH):
                pe.wait_ge(wi_landed[p], 16)
                for tb in range(NB):
                    if p == 0:
                        pe.wait_ge(xT_landed[tb], 16)
                    pe.wait_ge(tiles_by_act if tb < 2 else tiles_by_dve, p * 2 + tb % 2 + 1)
                    for k in range(KD):
                        ins = t_.matmul(bank[p % 2 * 4 + tb][:, 0:CW], xT[:, tb, k, :], wi[p][:, k, :],
                                        start=(k == 0), stop=(k == KD - 1))
                    ins.then_inc(tiles_ready, 1)
            with pe.Fori(0, QG_CH // WI_BUFS) as it:
                for i in range(WI_BUFS):
                    buf = (KV_CH + i) % WI_BUFS
                    pe.wait_ge(wi_landed[buf], (it + (KV_CH + i) // WI_BUFS + 1) * 16)
                    pe.wait_ge(tiles_by_act, it * WI_BUFS + (i + 2 * KV_CH + 3))
                    for k in range(KD):
                        ins = t_.matmul(bank[i % 2][:, 0:CW], xT[:, 0, k, :], wi[buf][:, k, :],
                                        start=(k == 0), stop=(k == KD - 1))
                    ins.then_inc(tiles_ready, 1)

            pe.wait_ge(keys_roped, NB)
            krot = work[:, 0:2560]
            for t in range(5):
                for kb in range(NB):
                    ins = t_.transpose(bank[2 + t][:, kb * P:(kb + 1) * P],
                                       krot[:, kb * 640 + t * P:kb * 640 + (t + 1) * P], ident[:])
                ins.then_inc(key_tiles_ready, 1)
            pe.wait_ge(kT_ready, 5)

            def landed(b, n):
                pe.wait_ge(w_landed[n % 2], 16 * (b * (N_W // 2) + n // 2 + 1))

            def two_tiles(src, done):
                for n in range(2):
                    for j in range(4):
                        ins = t_.transpose(bank[2 + n][:, j * P:(j + 1) * P], src[:, (4 * n + j) * P:(4 * n + j + 1) * P],
                                           ident[:])
                    ins.then_inc(done, 1)

            def scores(b, u):
                for m in softmaxes(u):
                    if m == 0:
                        pe.wait_ge(qT_ready, 2 * b + 2)
                    if m >= 2:
                        pe.wait_ge(probs_ready, b * NSM + m - 1)
                    if u < AH:
                        g, tile, ktile = u // 4, u % 4, 0
                    else:
                        g, tile, ktile = m % 2, 4 + (u - AH), 1 + (u - AH)
                    rows = slice(g * HD, (g + 1) * HD)
                    t_.matmul(bank[2 + m % 2][:], qT[rows, tile, :], kT[rows, ktile * T:(ktile + 1) * T],
                              start=True, stop=True).then_inc(scores_ready, 1)

            def attend(b, step):
                if step == 0:
                    scores(b, 0)
                if step + 1 < UNITS:
                    scores(b, step + 1)
                u = step - 1
                if 0 <= u < UNITS:
                    if u < AH:
                        pe.wait_ge(probs_ready, b * NSM + u + 1)
                    else:
                        pe.wait_ge(combined_ready, b * BH + u - AH + 1)
                    pu = probs[softmaxes(u)[0] % 4]
                    for j in range(NB):
                        ins = t_.transpose(bank[4 + u % 2][:, j * P:(j + 1) * P], pu[:, j * P:(j + 1) * P], ident[:])
                    ins.then_inc(pT_tiles_ready, 1)
                w = step - 2
                if 0 <= w < UNITS:
                    pe.wait_ge(pT_ready, b * UNITS + w + 1)
                    if w >= 2:
                        pe.wait_ge(o_taken, b * UNITS + w - 1)
                    width = HD if w < AH else 2 * HD
                    for kc in range(NB):
                        c0 = kc * COLS + (VA + (w // 4) * HD if w < AH else VB + (w - AH) * 2 * HD)
                        ins = t_.matmul(bank[6 + w % 2][:, 0:width], pT[w % 2][:, kc * P:(kc + 1) * P],
                                        proj[:, c0:c0 + width], start=(kc == 0), stop=(kc == NB - 1))
                    ins.then_inc(o_ready, 1)

            def stages(name, b):
                if name == "q_tiles":
                    pe.wait_ge(q_roped, 2 * b + 2)
                    if not isinstance(b, int) or b > 0:
                        pe.wait_ge(s_ready, 4 * b)
                    two_tiles(qrot, q_tiles_ready)
                elif name.startswith("attend"):
                    attend(b, int(name[6:]))
                elif name == "y_tiles":
                    pe.wait_ge(y_ready, b + 1)
                    two_tiles(yab, y_tiles_ready)
                elif name == "branches":
                    pe.wait_ge(yT_ready, 2 * b + 2)
                    for n in range(4):
                        landed(b, 2 + n)
                        w = wbuf[:, n % 2, :].rearrange("p (k c) -> p k c", k=4)
                        for k in range(4):
                            ins = t_.matmul(bank[4 + n][:], yT[:, 4 * (n % 2) + k, :], w[:, k, :],
                                            start=(k == 0), stop=(k == 3))
                        ins.then_inc(branch_ready, 1)
                elif name == "m_tiles":
                    pe.wait_ge(merged_ready, 2 * b + 2)
                    two_tiles(merged, m_tiles_ready)
                elif name == "outproj":
                    pe.wait_ge(mT_ready, 2 * b + 2)
                    for n in range(4):
                        landed(b, 6 + n)
                        w = wbuf[:, n % 2, :].rearrange("p (k c) -> p k c", k=KD)
                        for k in range(KD):
                            ins = t_.matmul(bank[4 + n // 2][:, n % 2 * 256:n % 2 * 256 + 256], mT[:, k, :], w[:, k, :],
                                            start=(k == 0), stop=(k == KD - 1))
                        ins.then_inc(outproj_ready, 1)
                elif name == "h_tiles":
                    pe.wait_ge(h_ready, b + 1)
                    two_tiles(h_new, h_tiles_ready)
                elif name.startswith("query"):
                    pe.wait_ge(hT_ready, 2 * b + 2)
                    for q in range(2 * int(name[-1]), 2 * int(name[-1]) + 2):
                        landed(b, 11 + q)
                        w = wbuf[:, (11 + q) % 2, :].rearrange("p (k c) -> p k c", k=KD)
                        for j in range(2):
                            ct = 2 * q + j
                            for k in range(KD):
                                ins = t_.matmul(bank[4 + ct // 4][:, ct % 4 * P:ct % 4 * P + P], w[:, k, j * P:(j + 1) * P],
                                                hT[:, k, :], start=(k == 0), stop=(k == KD - 1))
                        ins.then_inc(query_ready, 1)
                elif name == "key_scores":
                    landed(b, 19)
                    keys = wbuf[:, 1, :].rearrange("p (t n) -> p t n", t=HI)
                    pe.wait_ge(qqT_ready, 4 * b + 4)
                    for hi in range(HI):
                        ins = t_.matmul(bank[2 + hi // 4][:, hi % 4 * P:hi % 4 * P + P], qqT[:, hi, :], keys[:, hi, :],
                                        start=True, stop=True)
                        if hi % 4 == 3:
                            ins.then_inc(keyscores_ready, 1)

            def clear(c):
                pe.wait_ge(y_free, c + 1)
                for n in range(2):
                    t_.matmul(bank[n][:, 0:2], zeros[:], zeros[:, 0:2], start=True, stop=False, skip_group_check=True)

            def batch(c, g, bt):
                if isinstance(g, int) and g == 0 and bt == 0:
                    clear(c)
                G = c * GROUPS + g
                for k in range(bt * BATCH, (bt + 1) * BATCH, 2):
                    pe.wait_ge(diag_ready, G * (RING // 2) + k // 2 + 1)
                    for n in range(2):
                        ins = t_.matmul(bank[n][:], diag[:, k // 2, :], uv(k)[:, D + n * 512:D + (n + 1) * 512],
                                        start=False, stop=False, skip_group_check=True)
                    ins.then_inc(pe_slots_free, 1)

            pe.wait_ge(zeros_set, 1)
            in_order(stages, None, 0)
            clear(0)
            pe.wait_ge(s_ready, 4)
            pe.wait_ge(xT_late_landed, 16)
            with pe.Fori(0, LATE_GROUPS) as g:
                for j in range(2):
                    pe.wait_ge(late_landed[j], g * 16 + 16)
                    w = wbuf[:, j, :].rearrange("p (k c) -> p k c", k=KD)
                    for tb in range(1, NB):
                        pe.wait_ge(late_tiles_copied, (g * 2 + j) * LATE + tb)
                        for k in range(KD):
                            ins = t_.matmul(bank[1 + 3 * j + tb][:, 0:CW], xT_late[:, tb - 1, k, :], w[:, k, :],
                                            start=(k == 0), stop=(k == KD - 1))
                        ins.then_inc(late_tiles_ready, 1)
                    batch(0, g, j)
            in_order(stages, batch, 1, LATE_GROUPS * BPG)
            with pe.Fori(2, NB) as b:
                in_order(stages, batch, b)
            clear(NB - 1)
            with pe.Fori(0, GROUPS) as g:
                for bt in range(BPG):
                    batch(NB - 1, g, bt)


def rope_table():
    def table(pos, dim):
        freqs = np.float32(10000.0) ** (-np.arange(0, dim, 2, dtype=np.float32) / np.float32(dim))
        ang = pos.astype(np.float32)[:, None] * freqs[None, :]
        cos, sin = np.cos(ang), np.sin(ang)
        return np.concatenate([cos, cos], 1), np.concatenate([-sin, sin], 1)

    pos = np.arange(T)
    row, col, seq = table(pos // 64, HD // 2), table(pos % 64, HD // 2), table(pos, HD)
    a = [np.concatenate([row[i], col[i]], 1) for i in range(2)]
    out = np.stack([a[0], a[1], seq[0], seq[1]]).astype(np.float32)
    return np.ascontiguousarray(out.reshape(4, NB, P, HD).transpose(2, 0, 1, 3).reshape(P, 4, NB * HD))


def kernel(**inputs):
    import concourse.bacc as bacc
    from concourse.bass_utils import run_bass_kernel_spmd

    f = {k: np.asarray(a) for k, a in inputs.items()}
    x = f["x"][0]
    w_in = f["w_in"][0]
    qa = w_in[:, 0:512].reshape(D, 2, 4, HD).transpose(0, 2, 1, 3).reshape(D, 512)
    w_in = np.concatenate([w_in[:, 512:640], w_in[:, 1280:1792], w_in[:, 640:768], w_in[:, 1792:2304], qa,
                           w_in[:, 768:1280], w_in[:, 2304:]], axis=1)
    w_in = w_in.reshape(KD, P, NCH, CW).transpose(2, 1, 0, 3).reshape(NCH * P, KD * CW)

    def pieces(w, width):
        rows, cols = w.shape
        return list(w.reshape(rows // P, P, cols // width, width).transpose(2, 1, 0, 3).reshape(-1, P, 2048))

    a, b = pieces(f["w_proj_a"][0], 512), pieces(f["w_proj_b"][0], 512)
    keys = f["sub_keys"][0].transpose(3, 0, 1, 2).reshape(P, HI * NK)
    wch = np.stack([a[0], b[0], a[1], b[1]] + pieces(f["w_out"][0], 256) + pieces(f["w_query"][0], 256) + [keys])
    arrays = {
        "x": x,
        "xT": x.reshape(NB, P, KD, P).transpose(0, 3, 2, 1).reshape(NB, P, D),
        "w_in": w_in,
        "w_chunks": wch,
        "b_gate": f["b_gate"],
        "ln1": np.concatenate([f["ln1_g"], f["ln1_b"]], axis=1),
        "ln2": np.concatenate([f["ln2_g"], f["ln2_b"]], axis=1),
        "gains": np.concatenate([f["q_norm_a"], f["k_norm_a"]], axis=1),
        "subln": f["subln_b"],
        "lambdas": np.concatenate([f["lambda_q1"], f["lambda_k1"], f["lambda_q2"], f["lambda_k2"]], axis=1),
        "rope": rope_table(),
        "ident": np.eye(P, dtype=np.float32),
        "iota": np.arange(TOPK, dtype=np.float32)[None],
        "uv": np.concatenate([f["u_table"][0], f["v_table"][0]], axis=1),
    }
    arrays = {f"in_{k}": np.ascontiguousarray(a) for k, a in arrays.items()}
    nc = bacc.Bacc("TRN2", target_bir_lowering=False, num_devices=1)
    args = [nc.dram_tensor(k, a.shape, mybir.dt.from_np(a.dtype), kind="ExternalInput").ap() for k, a in arrays.items()]
    out = nc.dram_tensor("out", (T, D), F32, kind="ExternalOutput").ap()
    build(nc, *args, out)
    r = run_bass_kernel_spmd(nc, [arrays], core_ids=[0])
    return r.results[0]["out"].reshape(1, T, D)
```

```python
from contextlib import ExitStack

import numpy as np

import concourse.bass as bass
from concourse import mybir

F32 = mybir.dt.float32
U32 = mybir.dt.uint32
I32 = mybir.dt.int32
ALU = mybir.AluOpType
ACT = mybir.ActivationFunctionType
AX = mybir.AxisListType
ds = bass.ds

P = 128
T, D = 512, 1024
NB = T // P
KD = D // P
HD = 64
AH, BH = 8, 4
NS_A, NS_B = AH, 2 * BH
NSM = NS_A + NS_B
UNITS = AH + BH
KA, KB, VA, VB, QA, QB, GT, COLS = 0, 128, 640, 768, 1280, 1792, 2304, 4352
CW = 256
NCH = COLS // CW
KV_CH = QA // CW
Q_CH = (GT - QA) // CW
G_CH = NCH - KV_CH - Q_CH
QG_CH = Q_CH + G_CH
K_CH = -(-VA // CW)
WI_BUFS = 6
LATE = NB - 1
HEADS, NK, TOPK = 8, 128, 16
HI = 2 * HEADS
SLOTS = HEADS * TOPK
RING = 8
BATCH = 4
GROUPS = SLOTS // RING
BPG = RING // BATCH
ALPHA = 2.0 ** 0.25
LAMBDA_INIT = 0.8 - 0.6
EPS, LN_EPS = 1e-6, 1e-5
SCALE = HD ** -0.5
LOWEST = -3.0e38
GATE_W, BRANCH_W, OUT_W, LN1_W, QUERY_W, N_W = 0, 1, 5, 9, 10, 18
BUFFER = [0, 1, 2, 0, 1, 3, 2, 0, 1, 3, 2, 0, 1, 3, 2, 0, 1, 3]
W_BUFS = 4

DVE_STEPS = 199
BEGIN_STEPS = 4
FIN_STEPS = 8

A_STEPS = UNITS + 3
ORDER = ["G2", "rope", "D2", "q_tiles", "S2", "G3", "q_copy", "attend0", "late_tile0", "attend1", "late_tile1",
         "late_copy0", "G0", "attend2", "late_tile2", "late_copy1", "D1", "attend3", "late_tile3", "late_copy2",
         "S1", "D1", "attend4", "late_tile4", "late_copy3", "S1", "attend5", "late_tile5", "late_copy4", "D1",
         "attend6", "late_tile6", "late_copy5", "S1", "G1", "attend7", "late_tile7", "late_copy6", "attend8",
         "late_tile8", "late_copy7", "attend9", "late_tile9", "late_copy8", "G1", "D1", "attend10", "S1",
         "late_tile10", "late_copy9", "D1", "attend11", "late_tile11", "late_copy10", "S1", "attend12",
         "late_copy11", "D1", "attend13", "gates", "sigmoid", "S1", "attend14", "subln", "G2", "y_tiles",
         "y_copy", "G2", "branches", "G2", "merge", "G2", "m_tiles", "m_copy", "outproj", "G2", "G2", "ln1",
         "G2", "h_tiles", "h_copy", "query0", "G2", "qq_copy0", "keys0", "query1", "G2", "s_copy0", "qq_copy1",
         "keys1", "top0", "query2", "G2", "s_copy1", "qq_copy2", "keys2", "G2", "top1", "query3", "G2",
         "s_copy2", "qq_copy3", "keys3", "cand0", "G1", "best0", "s_copy3", "top2", "G1", "chooseA0", "exp0",
         "G0", "chooseB0", "chooseC0", "G1", "top3", "cand1", "G0", "best1", "G0", "chooseA1", "exp1", "G0",
         "chooseB1", "chooseC1", "G2"]
USED = "-xxxxxxxxxxx--x-x-x-x-x-x-x-x-x-"
BATCHES = SLOTS // BATCH


def is_batch(name):
    return name[0] in "GD"


assert sum(is_batch(name) for name in ORDER) == BATCHES == len(USED)
FIRST_ORDER = (["rope", "q_tiles", "q_copy"]
               + [x for u in range(A_STEPS) for x in ([f"attend{u}"] + ([f"gate_tile{u}"] if u < G_CH else [])
                                                      + ([f"gate_copy{u - 1}"] if 0 < u <= G_CH else []))]
               + ["subln", "y_tiles", "y_copy", "gates", "sigmoid", "branches", "merge", "m_tiles", "m_copy", "outproj",
                  "ln1", "h_tiles", "h_copy", "query0", "qq_copy0", "keys0", "query1", "s_copy0", "qq_copy1", "keys1",
                  "query2", "s_copy1", "top0", "qq_copy2", "keys2", "query3", "top1", "cand0", "best0", "s_copy2",
                  "qq_copy3", "keys3", "s_copy3", "chooseA0", "exp0", "chooseB0", "chooseC0", "begin", "top2", "E",
                  "top3", "cand1", "E", "best1", "E", "chooseA1", "exp1", "chooseB1", "E", "chooseC1", "begin_rest"])
EARLY_GROUPS = FIRST_ORDER.count("E") * BATCH // RING
LATE_GROUPS = 4
LOOP_CH = 2 * LATE_GROUPS
LATE_BY_DVE, LAST_BY_DVE = 3, 2
EARLY_BY_DVE = 0
DIAGS_BY_ACT = (0, 1)


def build(nc, x_d, xT_d, win_d, wch_d, bgate_d, ln1_d, ln2_d, gains_d, subln_d, lam_d, rope_d, ident_d, iota_d,
          uv_d, out_d):
    with ExitStack() as ctx:
        def sb(name, shape, dt=F32):
            return ctx.enter_context(nc.sbuf_tensor(name, shape, dt))

        def sem(name):
            return ctx.enter_context(nc.semaphore(name))

        bank = [ctx.enter_context(nc.psum_tensor(f"bank{i}", [P, 512], F32)) for i in range(8)]

        ring = sb("ring", [P, RING * 2 * D])
        proj = sb("proj", [P, NB * COLS])
        kT = sb("kT", [P, 5 * T])
        wbuf = sb("wbuf", [P, 2, 2048])
        work = sb("work", [P, 6144])
        h_new = sb("h_new", [P, D])
        h_cur = sb("h_cur", [P, D])
        diag = sb("diag", [P, RING // 2, P])
        y_dve = sb("y_dve", [P, D])
        ident = sb("ident", [P, P])
        zeros = sb("zeros", [P, P])
        rope = sb("rope", [P, 4, NB * HD])
        gains = sb("gains", [P, 2, HD])
        subln = sb("subln", [P, 2 * HD])
        iota16 = sb("iota16", [P, TOPK])
        lam_e = sb("lam_e", [P, 4])
        neg_lam = sb("neg_lam", [P, 1])
        ss = sb("ss", [P, 8])
        root = sb("root", [P, 8])
        rinv = sb("rinv", [P, 8])
        negmax = sb("negmax", [P, NSM])
        rsum = sb("rsum", [P, NSM])
        rs_inv = sb("rs_inv", [P, NSM])
        stats = sb("stats", [P, 2, 6])
        mv = sb("mv", [P, 2])
        fstats = sb("fstats", [P, 2, 6])
        fmv = sb("fmv", [P, 2])
        froot = sb("froot", [P, 1])
        sv = sb("sv", [P, HI, TOPK])
        si = sb("si", [P, HI, TOPK], U32)
        cv = sb("cv", [P, HEADS, TOPK])
        ci = sb("ci", [P, HEADS, TOPK], U32)
        gsum = sb("gsum", [P, HEADS])
        idx_new = sb("idx_new", [P, SLOTS], I32)
        idx_cur = sb("idx_cur", [P, SLOTS], I32)
        idx_slot = sb("idx_slot", [P, RING], I32)
        gate_new = sb("gate_new", [P, SLOTS])
        gate_cur = sb("gate_cur", [P, SLOTS])
        dots = sb("dots", [P, RING])
        gelu = sb("gelu", [P, RING])
        wts = sb("wts", [P, RING])

        def uv(k):
            return ring[:, k * 2 * D:(k + 1) * 2 * D]

        xT = ring[:, 0:KD * T].rearrange("p (b k t) -> p b k t", b=NB, k=KD)
        wi_flat = [ring[:, KD * T + i * KD * CW:KD * T + (i + 1) * KD * CW] for i in range(WI_BUFS)]
        wi = [piece.rearrange("p (k c) -> p k c", k=KD) for piece in wi_flat]

        def W(i, n=1024):
            return work[:, i * 1024:i * 1024 + n]

        assert COLS - QA == LATE * D
        xT_late = proj[:, QA:COLS].rearrange("p (b k t) -> p b k t", b=LATE, k=KD)
        diags = ([diag[:, i, :] for i in range(RING // 2)]
                 + [proj[:, i * COLS + 512:i * COLS + 512 + P] for i in range(RING // 2)])
        old_keys = proj[:].rearrange("p (b c) -> p b c", b=NB)[:, :, 0:512]

        whole = {0: wbuf[:, 0, :], 1: wbuf[:, 1, :], 3: proj[:, GT:GT + 2048]}

        def landed_count(b, n):
            uses = [m for m in range(N_W) if BUFFER[m] == BUFFER[n]]
            return w_landed[BUFFER[n]], 16 * (b * len(uses) + uses.index(n) + 1)

        def weights(n, k, width):
            c = k * width
            if BUFFER[n] != 2:
                return whole[BUFFER[n]][:, c:c + width]
            return proj[:, c // 512 * COLS + c % 512:c // 512 * COLS + c % 512 + width]

        sub_keys = [work[:, 5120:5632], work[:, 5632:6144]]
        qrot, qT = W(0), W(1).rearrange("p (t q) -> p t q", t=8)
        yT, mT = W(0).rearrange("p (t q) -> p t q", t=8), W(1).rearrange("p (t q) -> p t q", t=8)
        probs = [work[:, 2048 + 512 * i:2560 + 512 * i] for i in range(4)]
        pT = [work[:, 4096 + 512 * i:4608 + 512 * i] for i in range(2)]
        yab = W(5)
        merged, xblk = W(2), W(3)
        hT = W(4).rearrange("p (t q) -> p t q", t=8)
        qqT = W(2, 2048).rearrange("p (t q) -> p t q", t=HI)
        s = W(0, 2048).rearrange("p (t n) -> p t n", t=HI)
        cand = [W(2 + n).rearrange("p (h n) -> p h n", h=HEADS // 2) for n in range(2)]
        eq = [W(n).rearrange("p (k a) -> p k a", a=TOPK) for n in range(2)]

        def small(n, i, width=SLOTS // 2):
            return work[:, (2 + n) * 1024 + i * (SLOTS // 2):(2 + n) * 1024 + i * (SLOTS // 2) + width]

        ln2 = W(0, 2048)
        y_out = W(5)

        consts_landed = sem("consts_landed")
        zeros_set = sem("zeros_set")
        xT_landed = [sem(f"xT_landed{b}") for b in range(NB)]
        wi_landed = [sem(f"wi_landed{i}") for i in range(WI_BUFS)]
        tiles_ready = sem("tiles_ready")
        tiles_by_act = sem("tiles_by_act")
        tiles_by_dve = sem("tiles_by_dve")
        xT_late_landed = sem("xT_late_landed")
        late_landed = [sem("late_landed0"), sem("late_landed1")]
        late_tiles_ready = sem("late_tiles_ready")
        late_tiles_copied = sem("late_tiles_copied")
        key_meansq_ready = sem("key_meansq_ready")
        key_roots_ready = sem("key_roots_ready")
        keys_roped = sem("keys_roped")
        key_tiles_ready = sem("key_tiles_ready")
        kT_ready = sem("kT_ready")
        lam_dots_ready = sem("lam_dots_ready")
        lam_exp_ready = sem("lam_exp_ready")
        setup_step = sem("setup_step")
        w_landed = [sem(f"w_landed{i}") for i in range(W_BUFS)]
        sub_keys_landed = [sem("sub_keys_landed0"), sem("sub_keys_landed1")]
        x_landed = sem("x_landed")
        dve_step = sem("dve_step")
        meansq_ready = sem("meansq_ready")
        roots_ready = sem("roots_ready")
        gate_logits_ready = sem("gate_logits_ready")
        gates_ready = sem("gates_ready")
        q_roped = sem("q_roped")
        q_tiles_ready = sem("q_tiles_ready")
        qT_ready = sem("qT_ready")
        scores_ready = sem("scores_ready")
        negmax_ready = sem("negmax_ready")
        probs_ready = sem("probs_ready")
        combined_ready = sem("combined_ready")
        pT_tiles_ready = sem("pT_tiles_ready")
        pT_ready = sem("pT_ready")
        o_ready = sem("o_ready")
        o_taken = sem("o_taken")
        y_ready = sem("y_ready")
        y_tiles_ready = sem("y_tiles_ready")
        yT_ready = sem("yT_ready")
        branch_ready = sem("branch_ready")
        merged_ready = sem("merged_ready")
        m_tiles_ready = sem("m_tiles_ready")
        mT_ready = sem("mT_ready")
        outproj_ready = sem("outproj_ready")
        h_ready = sem("h_ready")
        h_tiles_ready = sem("h_tiles_ready")
        hT_ready = sem("hT_ready")
        query_ready = sem("query_ready")
        qqT_ready = sem("qqT_ready")
        keyscores_ready = sem("keyscores_ready")
        s_ready = sem("s_ready")
        cv_shifted = sem("cv_shifted")
        gate_exp_ready = sem("gate_exp_ready")
        chosen = sem("chosen")
        idx_taken = sem("idx_taken")
        idx_staged = sem("idx_staged")
        slot_free = [sem(f"slot_free{k}") for k in range(RING)]
        gather_step = sem("gather_step")
        waits_passed = sem("waits_passed")
        uv_landed = [sem(f"uv_landed{k}") for k in range(RING)]
        dots_ready = sem("dots_ready")
        gelu_ready = sem("gelu_ready")
        diags_ready = sem("diags_ready")
        y_free = sem("y_free")
        var_ready = sem("var_ready")
        froot_ready = sem("froot_ready")
        fin_step = sem("fin_step")
        begin_step = sem("begin_step")
        out_ready = sem("out_ready")
        out_stored = sem("out_stored")
        ln2_landed = sem("ln2_landed")

        N_CONSTS = 6
        block = ctx.enter_context(nc.Block())

        def softmaxes(u):
            return [u] if u < AH else [AH + 2 * (u - AH), AH + 2 * (u - AH) + 1]

        class Steps:
            def __init__(self, eng, semaphore, base):
                self.eng, self.sem, self.base, self.n = eng, semaphore, base, 0

            def did(self, ins):
                ins.then_inc(self.sem, 1)
                self.n += 1

            def wait(self):
                self.eng.wait_ge(self.sem, self.base + self.n)

            def pass_wait(self):
                self.wait()
                self.eng.sem_inc(waits_passed, 1)

            def alone(self, ins):
                self.did(ins)
                self.wait()

        def in_order(stage, dots_of, sums_of, b, done=0):
            n = done
            place = -1
            for name in ORDER:
                if name.startswith("late") and not done:
                    continue
                kind, by_dve = name[0], name[1:]
                if kind not in "GDS":
                    stage(name, b)
                    continue
                place += kind != "S"
                if done and USED[place] == "-":
                    continue
                if kind != "S":
                    dots_of(b - 1, n // BPG, n % BPG)
                    n += 1
                if kind != "D":
                    sums_of(b - 1, (n - 1) // BPG, (n - 1) % BPG, int(by_dve))
            assert n == BATCHES, n

        def first_block(stage, batch):
            n = 0
            for name in FIRST_ORDER:
                if name != "E":
                    stage(name, 0)
                    continue
                batch(0, n // BPG, n % BPG, EARLY_BY_DVE)
                n += 1

        def two_o_banks(b):
            return not isinstance(b, int) or b != 1

        def o_bank(b, u):
            return bank[6 + u % 2 if two_o_banks(b) else 6]

        def summed_by_dve(bt, n):
            return [bt * BATCH + k for k in ([], [3], [1, 3], [1, 2, 3])[n]]

        def tile_copied(p, tb):
            if p < K_CH:
                return (tiles_by_act if tb < 2 else tiles_by_dve, 2 * p + tb % 2 + 1)
            if p < KV_CH:
                return (tiles_by_act, 2 * K_CH + (p - K_CH) * NB + tb + 1)
            return (tiles_by_act, 2 * K_CH + (KV_CH - K_CH) * NB + p - KV_CH + 1)

        @block.sync
        def _(sp):
            def load_piece(p):
                sp.dma_start(wi_flat[p % WI_BUFS], win_d[p * P:(p + 1) * P, :]).then_inc(wi_landed[p % WI_BUFS], 16)

            for tb in range(NB):
                sp.dma_start(ring[:, tb * D:(tb + 1) * D], xT_d[tb]).then_inc(xT_landed[tb], 16)
                if tb == 0:
                    load_piece(0)
            for p in range(1, 3):
                load_piece(p)
            sp.dma_start(ident[:], ident_d).then_inc(consts_landed, 16)
            sp.dma_start(rope[:], rope_d).then_inc(consts_landed, 16)
            sp.dma_start(gains[:].rearrange("p a d -> p (a d)"), gains_d.to_broadcast([P, 2 * HD])).then_inc(consts_landed, 16)
            sp.dma_start(subln[:], subln_d.to_broadcast([P, 2 * HD])).then_inc(consts_landed, 16)
            sp.dma_start(iota16[:], iota_d.to_broadcast([P, TOPK])).then_inc(consts_landed, 16)
            sp.dma_start(W(5, 4 * HD), lam_d.to_broadcast([P, 4 * HD])).then_inc(consts_landed, 16)
            for p in range(3, NCH):
                if p >= WI_BUFS:
                    q = p - WI_BUFS
                    sp.wait_ge(tiles_ready, (q + 1) * NB if q < KV_CH else KV_CH * NB + q - KV_CH + 1)
                load_piece(p)

            release = ([(gate_logits_ready, 2, 2)]
                       + [(branch_ready, 4, n + 1) for n in range(4)]
                       + [(outproj_ready, 4, n + 1) for n in range(4)]
                       + [(h_ready, 1, 1)]
                       + [(query_ready, 8, n + 1) for n in range(8)])
            assert len(release) == N_W

            def load_sub_keys(b, n):
                if n == 0:
                    sp.wait_ge(merged_ready, 2 * b + 2)
                elif n >= 2:
                    sp.wait_ge(keyscores_ready, 4 * b + n - 1)
                sp.dma_start(sub_keys[n % 2], wch_d[N_W - 2][:, n * 512:(n + 1) * 512]).then_inc(sub_keys_landed[n % 2], 16)

            def stream(b, before):
                for n in range(N_W):
                    if n == BRANCH_W + 3:
                        sp.wait_ge(y_tiles_ready, 2 * b + 1)
                        sp.dma_start(xblk, x_d[ds(b * P, P), :]).then_inc(x_landed, 16)
                    if n == LN1_W:
                        load_sub_keys(b, 0)
                        load_sub_keys(b, 1)
                    if n == QUERY_W + 5:
                        load_sub_keys(b, 2)
                    if n == QUERY_W + 7:
                        load_sub_keys(b, 3)
                    held = [m for m in range(n) if BUFFER[m] == BUFFER[n]]
                    if held:
                        semaphore, per_block, count = release[held[-1]]
                        sp.wait_ge(semaphore, b * per_block + count)
                    elif before[BUFFER[n]] is not None:
                        sp.wait_ge(*before[BUFFER[n]])
                    landed = w_landed[BUFFER[n]]
                    if n == GATE_W:
                        sp.dma_start(wbuf[:, 0, :], bgate_d.to_broadcast([P, 2 * D])).then_inc(landed, 16)
                    elif n == LN1_W:
                        sp.dma_start(whole[BUFFER[n]], ln1_d.to_broadcast([P, 2 * D])).then_inc(landed, 16)
                    elif BUFFER[n] == 2:
                        sp.dma_start(old_keys, wch_d[n - 1 - (n > LN1_W)].rearrange("p (b c) -> p b c", b=NB)
                                     ).then_inc(landed, 16)
                    else:
                        sp.dma_start(whole[BUFFER[n]], wch_d[n - 1 - (n > LN1_W)]).then_inc(landed, 16)

            def store(c):
                sp.wait_ge(out_ready, c + 1)
                sp.dma_start(out_d[ds(c * P, P), :], y_out).then_inc(out_stored, 16)

            sp.sem_inc(out_stored, 16)
            stream(0, [None, None, (keys_roped, NB), (merged_ready, 2)])
            sp.wait_ge(query_ready, 8)
            sp.dma_start(proj[:, QA:COLS].rearrange("p (b c) -> p b c", b=LATE),
                         xT_d[1:NB].rearrange("b p c -> p b c")).then_inc(xT_late_landed, 16)
            for j in range(2):
                sp.wait_ge(query_ready, 6 + j)
                sp.dma_start(wbuf[:, j, :], win_d[(KV_CH + j) * P:(KV_CH + j + 1) * P, :]).then_inc(late_landed[j], 16)
            with sp.Fori(1, QG_CH // 2) as it:
                for j in range(2):
                    sp.wait_ge(late_tiles_ready, (it * 2 + j - 1) * LATE)
                    sp.dma_start(wbuf[:, j, :], win_d[ds((it * 2 + KV_CH + j) * P, P), :]).then_inc(late_landed[j], 16)

            def round_(b, before):
                stream(b, before)
                sp.wait_ge(chosen, 2 * b + 2)
                sp.dma_start(ln2, ln2_d.to_broadcast([P, 2 * D])).then_inc(ln2_landed, 16)
                store(b - 1)

            round_(1, [(late_tiles_ready, (QG_CH - 1) * LATE), (late_tiles_ready, QG_CH * LATE), (query_ready, 5),
                       (late_tiles_ready, QG_CH * LATE)])
            with sp.Fori(2, NB) as b:
                round_(b, [(query_ready, b * 8 - 2), (query_ready, b * 8 - 1), (query_ready, b * 8 - 3),
                           (query_ready, b * 8)])
            store(NB - 1)
            sp.wait_ge(out_stored, 16 * (NB + 1))

        @block.gpsimd
        def _(pool):
            nc.gpsimd.memset(zeros[:], 0.0).then_inc(zeros_set, 1)
            pool.wait_ge(tiles_ready, KV_CH * NB + QG_CH)

            def take(c, half):
                cols = slice(half * SLOTS // 2, (half + 1) * SLOTS // 2)
                pool.wait_ge(chosen, 2 * c + half + 1)
                pool.sem_inc(waits_passed, 1)
                nc.gpsimd.tensor_copy(idx_cur[:, cols], idx_new[:, cols]).then_inc(idx_taken, 1)
                pool.wait_ge(idx_taken, 2 * c + half + 1)
                pool.sem_inc(waits_passed, 1)

            def group(G, g):
                for k in range(RING):
                    pool.wait_ge(slot_free[k], G + 1)
                    if k % BATCH == 0:
                        nc.gpsimd.tensor_copy(idx_slot[:, k:k + BATCH],
                                              idx_cur[:, ds(g * RING + k, BATCH)]).then_inc(idx_staged, 1)
                        pool.wait_ge(idx_staged, G * (RING // BATCH) + k // BATCH + 1)
                    pool.sem_inc(waits_passed, 1)
                    nc.gpsimd.indirect_dma_start(
                        out=uv(k), out_offset=None, in_=uv_d,
                        in_offset=bass.IndirectOffsetOnAxis(ap=idx_slot[:, k:k + 1], axis=0)).then_inc(uv_landed[k], 16)

            with pool.Fori(0, NB) as c:
                for half in range(2):
                    take(c, half)
                    with pool.Fori(half * GROUPS // 2, (half + 1) * GROUPS // 2) as g:
                        group(c * GROUPS + g, g)

        @block.vector
        def _(dve):
            v = nc.vector
            dve.sem_inc(y_free, 1)
            for p in range(K_CH):
                for tb in (2, 3):
                    dve.wait_ge(tiles_ready, p * NB + tb + 1)
                    v.tensor_copy(proj[:, tb * COLS + p * CW:tb * COLS + (p + 1) * CW],
                                  bank[p % 2 * 4 + tb][:, 0:CW]).then_inc(tiles_by_dve, 1)

            setup = Steps(dve, setup_step, 0)

            def rope_tables(kind, b):
                return rope[:, 2 * kind, ds(b * HD, HD)], rope[:, 2 * kind + 1, ds(b * HD, HD)]

            def rotate(steps, out, x, tmp, n, kind, b, last):
                cos, sin = rope_tables(kind, b)
                parts = 2 if kind == 0 else 1
                half = HD // parts // 2
                m = n * parts
                hv = "p (m s d) -> p m s d"
                x4 = x.rearrange(hv, m=m, s=2)
                t4 = tmp.rearrange(hv, m=m, s=2)
                s4 = sin.rearrange("p (a s d) -> p a s d", a=parts, s=2)
                for side in range(2):
                    if kind == 0:
                        o_ap = t4[:, :, side, :].rearrange("p (n a) d -> p n a d", a=2)
                        x_ap = x4[:, :, 1 - side, :].rearrange("p (n a) d -> p n a d", a=2)
                        s_ap = s4[:, :, side, :].unsqueeze(1).to_broadcast([P, n, 2, half])
                    else:
                        o_ap, x_ap = t4[:, :, side, :], x4[:, :, 1 - side, :]
                        s_ap = s4[:, 0, side, :].unsqueeze(1).to_broadcast([P, n, half])
                    steps.did(v.tensor_tensor(o_ap, x_ap, s_ap, ALU.mult))
                hx = "p (n d) -> p n d"
                steps.alone(v.tensor_tensor(out.rearrange(hx, n=n), x.rearrange(hx, n=n),
                                            cos.unsqueeze(1).to_broadcast([P, n, HD]), ALU.mult))
                ins = v.tensor_tensor(out, out, tmp, ALU.add)
                if last is None:
                    steps.did(ins)
                else:
                    ins.then_inc(last, 1)

            dve.wait_ge(tiles_by_act, 2 * K_CH)
            dve.wait_ge(tiles_by_dve, 2 * K_CH)
            dve.wait_ge(consts_landed, 16 * N_CONSTS)
            krot = work[:, 0:2560]
            sq, ktmp, ky = work[:, 2560:3072], work[:, 3072:3584], work[:, 3584:4096]
            ka = proj[:].rearrange("p (b c) -> p b c", b=NB)[:, :, KA:KA + 2 * HD]
            setup.alone(v.tensor_tensor(sq.rearrange("p (b c) -> p b c", b=NB), ka, ka, ALU.mult))
            setup.alone(v.tensor_reduce(ss[:], sq.rearrange("p (n d) -> p n d", d=HD), AX.X, ALU.add))
            v.tensor_scalar(ss[:], ss[:], 1.0 / HD, EPS, ALU.mult, ALU.add).then_inc(key_meansq_ready, 1)
            lam = W(5, 4 * HD).rearrange("p (a d) -> p a d", a=4)
            lam_prod = work[:, 5120 + 4 * HD:5120 + 6 * HD].rearrange("p (a d) -> p a d", a=2)
            for a in range(2):
                setup.did(v.tensor_tensor(lam_prod[:, a, :], lam[:, 2 * a, :], lam[:, 2 * a + 1, :], ALU.mult))
            setup.wait()
            v.tensor_reduce(lam_e[:, 0:2], lam_prod, AX.X, ALU.add).then_inc(lam_dots_ready, 1)
            setup.did(v.tensor_scalar(subln[:], subln[:], 1.0 - LAMBDA_INIT, None, ALU.mult))
            dve.wait_ge(lam_exp_ready, 1)
            setup.alone(v.tensor_tensor(neg_lam[:], lam_e[:, 3:4], lam_e[:, 2:3], ALU.subtract))
            setup.alone(v.tensor_scalar(neg_lam[:], neg_lam[:], -LAMBDA_INIT, None, ALU.add))
            dve.wait_ge(key_roots_ready, 1)
            setup.alone(v.reciprocal(rinv[:], root[:]))
            for kb in range(NB):
                base = kb * COLS
                k3 = proj[:, base + KA:base + KA + 2 * HD].rearrange("p (n d) -> p n d", n=2)
                y3 = ky[:, 0:2 * HD].rearrange("p (n d) -> p n d", n=2)
                setup.alone(v.tensor_tensor(y3, k3, rinv[:, 2 * kb:2 * kb + 2].unsqueeze(2).to_broadcast([P, 2, HD]),
                                            ALU.mult))
                setup.alone(v.tensor_tensor(y3, y3, gains[:, 1, :].unsqueeze(1).to_broadcast([P, 2, HD]), ALU.mult))
                out = krot[:, kb * 640:(kb + 1) * 640]
                rotate(setup, out[:, 0:128], ky[:, 0:128], ktmp[:, 0:128], 2, 0, kb, None)
                setup.wait()
                rotate(setup, out[:, 128:640], proj[:, base + KB:base + KB + 512], ktmp, 8, 1, kb, keys_roped)
                setup.wait()

            def root_of(steps, b, which, src, n, scale, eps):
                v.tensor_scalar(ss[:, 0:n], src, scale, eps, ALU.mult, ALU.add).then_inc(meansq_ready, 1)
                dve.wait_ge(roots_ready, 3 * b + which + 1)
                steps.alone(v.reciprocal(rinv[:, 0:n], root[:, 0:n]))

            hold = {}

            def landed(b, n):
                dve.wait_ge(*landed_count(b, n))

            def top16(steps, vals, best, index, rows):
                for j in rows:
                    steps.did(v.max(best(j)[:, 0:8], vals(j)))
                steps.pass_wait()
                for j in rows:
                    steps.did(v.max_index(index(j)[:, 0:8], best(j)[:, 0:8], vals(j)))
                for j in rows:
                    steps.did(v.match_replace(vals(j), best(j)[:, 0:8], vals(j), LOWEST))
                steps.pass_wait()
                for j in rows:
                    steps.did(v.max(best(j)[:, 8:16], vals(j)))
                steps.pass_wait()
                for j in rows:
                    steps.did(v.max_index(index(j)[:, 8:16], best(j)[:, 8:16], vals(j)))

            def attend(b, step):
                steps = hold["steps"]
                if step < UNITS:
                    for m in softmaxes(step):
                        dve.wait_ge(scores_ready, b * NSM + m + 1)
                        v.tensor_reduce(negmax[:, m:m + 1], bank[2 + m % 2][:], AX.X, ALU.max,
                                        negate=True).then_inc(negmax_ready, 1)
                u = step - 1
                if AH <= u < UNITS:
                    m0, m1 = softmaxes(u)
                    dve.wait_ge(probs_ready, b * NSM + m1 + 1)
                    steps.alone(v.reciprocal(rs_inv[:, m0:m1 + 1], rsum[:, m0:m1 + 1]))
                    steps.did(v.tensor_scalar(probs[m0 % 4], probs[m0 % 4], rs_inv[:, m0:m0 + 1], None, ALU.mult))
                    steps.alone(v.tensor_scalar(rs_inv[:, m1:m1 + 1], rs_inv[:, m1:m1 + 1],
                                                neg_lam[:, 0:1], None, ALU.mult))
                    v.scalar_tensor_tensor(probs[m0 % 4], probs[m1 % 4], rs_inv[:, m1:m1 + 1], probs[m0 % 4],
                                           ALU.mult, ALU.add).then_inc(combined_ready, 1)
                u = step - 3
                if 0 <= u < AH:
                    dve.wait_ge(probs_ready, b * NSM + u + 1)
                    steps.alone(v.reciprocal(rs_inv[:, u:u + 1], rsum[:, u:u + 1]))
                    dve.wait_ge(o_ready, b * UNITS + u + 1)
                    v.tensor_scalar(yab[:, u * HD:(u + 1) * HD], o_bank(b, u)[:, 0:HD],
                                    rs_inv[:, u:u + 1], None, ALU.mult).then_inc(o_taken, 1)
                elif AH <= u < UNITS:
                    dve.wait_ge(o_ready, b * UNITS + u + 1)
                    c0 = AH * HD + (u - AH) * 2 * HD
                    v.tensor_copy(yab[:, c0:c0 + 2 * HD], o_bank(b, u)[:, 0:2 * HD]).then_inc(o_taken, 1)

            def stages(name, b):
                if name == "rope":
                    hold["steps"] = Steps(dve, dve_step, b * DVE_STEPS)
                steps = hold["steps"]
                if name == "gates":
                    if isinstance(b, int) and b == 1:
                        dve.wait_ge(late_tiles_copied, (QG_CH + 2) * LATE)
                    elif isinstance(b, int):
                        dve.wait_ge(*tile_copied(NCH - 1, 0))
                    landed(b, GATE_W)
                    for n in range(2):
                        g = proj[:, ds(b * COLS + GT + n * D, D)]
                        v.tensor_tensor(g, g, wbuf[:, 0, n * D:(n + 1) * D], ALU.add).then_inc(gate_logits_ready, 1)
                elif name == "rope":
                    if isinstance(b, int):
                        dve.wait_ge(*((late_tiles_copied, (LOOP_CH + 2) * LATE) if b else tile_copied(KV_CH + Q_CH - 1, 0)))
                    if isinstance(b, int) and b == 0:
                        dve.wait_ge(keys_roped, NB)
                        dve.wait_ge(key_tiles_ready, 5)
                    else:
                        dve.wait_ge(out_stored, b * 16)
                    q = proj[:, ds(b * COLS + QA, 512)]
                    sq, qy, tmp = W(2, 512), W(3, 512), W(4, 512)
                    hx = "p (n d) -> p n d"
                    steps.alone(v.tensor_tensor(sq, q, q, ALU.mult))
                    steps.alone(v.tensor_reduce(ss[:], sq.rearrange(hx, n=AH), AX.X, ALU.add))
                    root_of(steps, b, 0, ss[:], AH, 1.0 / HD, EPS)
                    steps.alone(v.tensor_tensor(qy.rearrange(hx, n=AH), q.rearrange(hx, n=AH),
                                                rinv[:].unsqueeze(2).to_broadcast([P, AH, HD]), ALU.mult))
                    steps.alone(v.tensor_tensor(qy.rearrange(hx, n=AH), qy.rearrange(hx, n=AH),
                                                gains[:, 0, :].unsqueeze(1).to_broadcast([P, AH, HD]), ALU.mult))
                    rotate(steps, qrot[:, 0:512], qy, tmp, AH, 0, b, q_roped)
                    rotate(steps, qrot[:, 512:1024], proj[:, ds(b * COLS + QB, 512)], W(5, 512), NS_B, 1, b, q_roped)
                elif name.startswith("attend"):
                    attend(b, int(name[6:]))
                elif name == "subln":
                    dve.wait_ge(o_taken, (b + 1) * UNITS)
                    yb = yab[:, 512:1024]
                    sq = W(3, 512)
                    hx = "p (n d) -> p n d"
                    steps.alone(v.tensor_tensor(sq, yb, yb, ALU.mult))
                    steps.alone(v.tensor_reduce(ss[:, 0:BH], sq.rearrange(hx, n=BH), AX.X, ALU.add))
                    root_of(steps, b, 1, ss[:, 0:BH], BH, 1.0 / (2 * HD), EPS)
                    steps.alone(v.tensor_tensor(yb.rearrange(hx, n=BH), yb.rearrange(hx, n=BH),
                                                rinv[:, 0:BH].unsqueeze(2).to_broadcast([P, BH, 2 * HD]), ALU.mult))
                    v.tensor_tensor(yb.rearrange(hx, n=BH), yb.rearrange(hx, n=BH),
                                    subln[:].unsqueeze(1).to_broadcast([P, BH, 2 * HD]), ALU.mult).then_inc(y_ready, 1)
                elif name == "merge":
                    dve.wait_ge(gates_ready, 2 * b + 2)
                    for n in range(2):
                        gA = proj[:, ds(b * COLS + GT + n * 512, 512)]
                        gB = proj[:, ds(b * COLS + GT + D + n * 512, 512)]
                        m, t = merged[:, n * 512:(n + 1) * 512], yab[:, n * 512:(n + 1) * 512]
                        dve.wait_ge(branch_ready, 4 * b + 2 * n + 1)
                        steps.did(v.tensor_tensor(m, gA, bank[4 + 2 * n][:], ALU.mult))
                        dve.wait_ge(branch_ready, 4 * b + 2 * n + 2)
                        steps.alone(v.tensor_tensor(t, gB, bank[5 + 2 * n][:], ALU.mult))
                        v.tensor_tensor(m, m, t, ALU.add).then_inc(merged_ready, 1)
                elif name == "ln1":
                    dve.wait_ge(x_landed, 16 * (b + 1))
                    for n in range(2):
                        c = slice(n * 512, (n + 1) * 512)
                        dve.wait_ge(outproj_ready, 4 * b + 2 * n + 2)
                        steps.alone(v.scalar_tensor_tensor(h_new[:, c], xblk[:, c], ALPHA, bank[4 + n][:],
                                                           ALU.mult, ALU.add))
                        steps.did(v.bn_stats(stats[:, n, :], h_new[:, c]))
                    steps.pass_wait()
                    steps.alone(v.bn_aggr(mv[:], stats[:]))
                    root_of(steps, b, 2, mv[:, 1:2], 1, 1.0, LN_EPS)
                    steps.alone(v.tensor_scalar(h_new[:], h_new[:], mv[:, 0:1], rinv[:, 0:1], ALU.subtract, ALU.mult))
                    landed(b, LN1_W)
                    steps.alone(v.tensor_tensor(h_new[:], h_new[:], whole[BUFFER[LN1_W]][:, 0:D], ALU.mult))
                    v.tensor_tensor(h_new[:], h_new[:], whole[BUFFER[LN1_W]][:, D:2 * D], ALU.add).then_inc(h_ready, 1)
                elif name.startswith("top"):
                    n = int(name[-1])
                    dve.wait_ge(s_ready, 4 * b + n + 1)
                    dve.sem_inc(waits_passed, 1)
                    top16(steps, lambda j: s[:, j, :], lambda j: sv[:, j, :], lambda j: si[:, j, :],
                          range(4 * n, 4 * n + 4))
                elif name.startswith("cand"):
                    n = int(name[-1])
                    steps.wait()
                    sv4 = sv[:].rearrange("p (h i) k -> p h i k", i=2)[:, 4 * n:4 * n + 4]
                    steps.alone(v.tensor_tensor(
                        cand[n].rearrange("p h (a b) -> p h a b", a=TOPK),
                        sv4[:, :, 0, :].unsqueeze(3).to_broadcast([P, 4, TOPK, TOPK]),
                        sv4[:, :, 1, :].unsqueeze(2).to_broadcast([P, 4, TOPK, TOPK]), ALU.add))
                elif name.startswith("best"):
                    steps.pass_wait()
                    n = int(name[-1])
                    top16(steps, lambda j: cand[n][:, j - 4 * n, :], lambda j: cv[:, j, :], lambda j: ci[:, j, :],
                          range(4 * n, 4 * n + 4))
                elif name.startswith("choose"):
                    choose(steps, b, name[-2], int(name[-1]))
                elif name == "begin":
                    begin(b)
                elif name == "begin_rest":
                    begin_rest()

            def choose(steps, b, part, n):
                hs = slice(n * 4, n * 4 + 4)
                half = SLOTS // 2
                cols = slice(n * half, (n + 1) * half)
                pa, pb = small(n, 0).bitcast(U32), small(n, 1).bitcast(U32)
                paf, pbf, e1, e2 = [small(n, i) for i in (2, 3, 4, 5)]
                sif = small(n, 6, SLOTS).rearrange("p (h i k) -> p h i k", h=4, i=2)
                if part == "A":
                    steps.wait()
                    steps.alone(v.tensor_copy(gsum[:, hs], cv[:, hs, 0]))
                    v.tensor_tensor(cv[:, hs, :], cv[:, hs, :], gsum[:, hs].unsqueeze(2).to_broadcast([P, 4, TOPK]),
                                    ALU.subtract).then_inc(cv_shifted, 1)
                    cif = ci[:, hs, :].rearrange("p h k -> p (h k)")
                    steps.did(v.tensor_scalar(pa, cif, 4, None, ALU.logical_shift_right))
                    steps.did(v.tensor_scalar(pb, cif, TOPK - 1, None, ALU.bitwise_and))
                    steps.alone(v.tensor_copy(sif, si[:, 8 * n:8 * n + 8, :].rearrange("p (h i) k -> p h i k", i=2)))
                    steps.did(v.tensor_copy(paf, pa))
                    steps.alone(v.tensor_copy(pbf, pb))
                    return
                pf, e, i = (paf, e1, 0) if part == "B" else (pbf, e2, 1)
                steps.alone(v.tensor_tensor(eq[n], pf.unsqueeze(2).to_broadcast([P, half, TOPK]),
                                            iota16[:].unsqueeze(1).to_broadcast([P, half, TOPK]), ALU.is_equal))
                eq4 = eq[n].rearrange("p (h k) a -> p h k a", h=4)
                steps.alone(v.tensor_tensor(eq4, eq4, sif[:, :, i, :].unsqueeze(2).to_broadcast([P, 4, TOPK, TOPK]),
                                            ALU.mult))
                steps.alone(v.tensor_reduce(e, eq[n], AX.X, ALU.add))
                if part == "B":
                    return
                dve.wait_ge(gate_exp_ready, 2 * b + n + 1)
                steps.alone(v.tensor_reduce(gsum[:, hs], cv[:, hs, :], AX.X, ALU.add))
                steps.alone(v.reciprocal(gsum[:, hs], gsum[:, hs]))
                steps.did(v.tensor_tensor(gate_new[:, cols].rearrange("p (h k) -> p h k", h=4), cv[:, hs, :],
                                          gsum[:, hs].unsqueeze(2).to_broadcast([P, 4, TOPK]), ALU.mult))
                if not isinstance(b, int) or b > 0:
                    dve.wait_ge(idx_taken, 2 * b + n - 1)
                v.scalar_tensor_tensor(idx_new[:, cols], e1, float(NK), e2, ALU.mult, ALU.add).then_inc(chosen, 1)
                if n == 1:
                    assert steps.n == DVE_STEPS, steps.n

            def dots_of(c, g, bt):
                G = c * GROUPS + g
                ks = range(bt * BATCH, (bt + 1) * BATCH)
                for k in ks:
                    dve.wait_ge(uv_landed[k], (G + 1) * 16)
                    u = uv(k)[:, 0:D]
                    ins = v.tensor_tensor_reduce(out=u, in0=u, in1=h_cur[:], scale=1.0, scalar=0.0, op0=ALU.mult,
                                                 op1=ALU.add, accum_out=dots[:, k:k + 1])
                ins.then_inc(dots_ready, 1)

            def sums_of(c, g, bt, by_dve):
                G = c * GROUPS + g
                B = G * BPG + bt
                ks = range(bt * BATCH, (bt + 1) * BATCH)
                steps = Steps(dve, gather_step, B)
                dve.wait_ge(gelu_ready, B + 1)
                sl = slice(bt * BATCH, (bt + 1) * BATCH)
                steps.alone(v.tensor_tensor(wts[:, sl], gelu[:, sl], gate_cur[:, ds(g * RING + bt * BATCH, BATCH)],
                                            ALU.mult))
                own = summed_by_dve(bt, by_dve)
                if by_dve not in DIAGS_BY_ACT:
                    for k in ks:
                        if k not in own:
                            dve.wait_ge(slot_free[k], G + 1)
                            ins = v.tensor_scalar(diags[k], ident[:], wts[:, k:k + 1], None, ALU.mult)
                    ins.then_inc(diags_ready, 1)
                for k in own:
                    v.scalar_tensor_tensor(y_dve[:], uv(k)[:, D:2 * D], wts[:, k:k + 1], y_dve[:],
                                           ALU.mult, ALU.add).then_inc(slot_free[k], 1)
                    dve.wait_ge(slot_free[k], G + 2)

            def batch(c, g, bt, by_dve):
                dots_of(c, g, bt)
                sums_of(c, g, bt, by_dve)

            def begin(b):
                hold["steps"].wait()
                steps = hold["begin"] = Steps(dve, begin_step, b * BEGIN_STEPS)
                steps.did(v.memset(y_dve[:], 0.0))
                steps.did(v.tensor_copy(gate_cur[:, 0:SLOTS // 2], gate_new[:, 0:SLOTS // 2]))
                steps.alone(v.tensor_copy(h_cur[:], h_new[:]))

            def begin_rest():
                hold["steps"].wait()
                steps = hold["begin"]
                steps.alone(v.tensor_copy(gate_cur[:, SLOTS // 2:], gate_new[:, SLOTS // 2:]))
                assert steps.n == BEGIN_STEPS, steps.n

            def add_up(c):
                steps = Steps(dve, fin_step, c * FIN_STEPS)
                for k in range(RING):
                    dve.wait_ge(slot_free[k], (c + 1) * GROUPS + 1)
                for n in range(2):
                    col = slice(n * 512, (n + 1) * 512)
                    steps.did(v.scalar_tensor_tensor(y_out[:, col], h_cur[:, col], ALPHA, bank[n][:], ALU.mult, ALU.add))
                steps.wait()
                v.tensor_tensor(y_out, y_out, y_dve[:], ALU.add).then_inc(y_free, 1)
                dve.wait_ge(y_free, c + 2)
                return steps

            def finish(c, steps):
                for n in range(2):
                    steps.did(v.bn_stats(fstats[:, n, :], y_out[:, n * 512:(n + 1) * 512]))
                steps.pass_wait()
                steps.alone(v.bn_aggr(fmv[:], fstats[:]))
                v.tensor_scalar(fmv[:, 1:2], fmv[:, 1:2], LN_EPS, None, ALU.add).then_inc(var_ready, 1)
                dve.wait_ge(froot_ready, c + 1)
                steps.alone(v.reciprocal(froot[:], froot[:]))
                steps.alone(v.tensor_scalar(y_out, y_out, fmv[:, 0:1], froot[:, 0:1], ALU.subtract, ALU.mult))
                dve.wait_ge(ln2_landed, 16 * (NB - 1) if isinstance(c, int) and c == NB - 1 else (c + 1) * 16)
                steps.alone(v.tensor_tensor(y_out, y_out, ln2[:, 0:D], ALU.mult))
                v.tensor_tensor(y_out, y_out, ln2[:, D:2 * D], ALU.add).then_inc(out_ready, 1)
                assert steps.n == FIN_STEPS, steps.n

            first_block(stages, batch)

            def round_(b, done):
                in_order(stages, dots_of, sums_of, b, done)
                steps = add_up(b - 1)
                begin(b)
                begin_rest()
                finish(b - 1, steps)

            with dve.Fori(0, LATE_GROUPS) as g:
                for bt in range(BPG):
                    batch(0, g + EARLY_GROUPS, bt, LATE_BY_DVE)
            round_(1, (EARLY_GROUPS + LATE_GROUPS) * BPG)
            with dve.Fori(2, NB) as b:
                round_(b, 0)
            with dve.Fori(0, GROUPS) as g:
                for bt in range(BPG):
                    batch(NB - 1, g, bt, LAST_BY_DVE)
            dve.wait_ge(out_stored, 16 * NB)
            finish(NB - 1, add_up(NB - 1))

        @block.scalar
        def _(act):
            a = nc.scalar
            act.sem_inc(late_tiles_copied, 2 * LATE)
            for p in range(KV_CH):
                for tb in range(2 if p < K_CH else NB):
                    act.wait_ge(tiles_ready, p * NB + tb + 1)
                    a.activation(proj[:, tb * COLS + p * CW:tb * COLS + (p + 1) * CW],
                                 bank[p % 2 * 4 + tb][:, 0:CW], ACT.Copy).then_inc(tiles_by_act, 1)
                if p == K_CH:
                    act.wait_ge(key_meansq_ready, 1)
                    a.activation(root[:], ss[:], ACT.Sqrt).then_inc(key_roots_ready, 1)
                    act.wait_ge(lam_dots_ready, 1)
                    a.activation(lam_e[:, 2:4], lam_e[:, 0:2], ACT.Exp).then_inc(lam_exp_ready, 1)

            def copy_first_block(n):
                act.wait_ge(tiles_ready, KV_CH * NB + n + 1)
                a.activation(proj[:, QA + n * CW:QA + (n + 1) * CW],
                             bank[4 + n if n < Q_CH else (n - Q_CH) % 2][:, 0:CW], ACT.Copy).then_inc(tiles_by_act, 1)

            for n in range(Q_CH):
                copy_first_block(n)
            for t in range(5):
                act.wait_ge(key_tiles_ready, t + 1)
                a.activation(kT[:, t * T:(t + 1) * T], bank[2 + t][:], ACT.Copy).then_inc(kT_ready, 1)

            def take_root(b, which, n):
                act.wait_ge(meansq_ready, 3 * b + which + 1)
                a.activation(root[:, 0:n], ss[:, 0:n], ACT.Sqrt).then_inc(roots_ready, 1)

            def two_tiles(b, asked, done, dst, scale=1.0):
                for n in range(2):
                    act.wait_ge(asked, 2 * b + n + 1)
                    a.activation(dst[:, 4 * n:4 * n + 4, :].rearrange("p t q -> p (t q)"), bank[2 + n][:],
                                 ACT.Copy, scale=scale).then_inc(done, 1)

            def attend(b, step):
                u = step - 2
                if 0 <= u < UNITS:
                    act.wait_ge(pT_tiles_ready, b * UNITS + u + 1)
                    a.activation(pT[u % 2], bank[4 + u % 2][:], ACT.Copy).then_inc(pT_ready, 1)
                if step < UNITS:
                    for m in softmaxes(step):
                        act.wait_ge(negmax_ready, b * NSM + m + 1)
                        a.activation(probs[m % 4], bank[2 + m % 2][:], ACT.Exp, bias=negmax[:, m:m + 1],
                                     accum_out=rsum[:, m:m + 1]).then_inc(probs_ready, 1)

            def stages(name, b):
                if name == "sigmoid":
                    for n in range(2):
                        act.wait_ge(gate_logits_ready, 2 * b + n + 1)
                        g = proj[:, ds(b * COLS + GT + n * D, D)]
                        a.activation(g, g, ACT.Sigmoid).then_inc(gates_ready, 1)
                elif name == "rope":
                    take_root(b, 0, AH)
                elif name == "q_copy":
                    two_tiles(b, q_tiles_ready, qT_ready, qT, SCALE)
                elif name.startswith("late_copy"):
                    n = int(name[9:])
                    act.wait_ge(late_tiles_ready, LOOP_CH * LATE + n + 1)
                    c0 = (1 + n % LATE) * COLS + QA + (LOOP_CH + n // LATE) * CW
                    a.activation(proj[:, c0:c0 + CW], bank[7][:, 0:CW], ACT.Copy).then_inc(late_tiles_copied, 1)
                elif name.startswith("gate_copy"):
                    copy_first_block(Q_CH + int(name[9:]))
                elif name.startswith("attend"):
                    attend(b, int(name[6:]))
                elif name == "subln":
                    take_root(b, 1, BH)
                elif name == "y_copy":
                    two_tiles(b, y_tiles_ready, yT_ready, yT)
                elif name == "m_copy":
                    two_tiles(b, m_tiles_ready, mT_ready, mT)
                elif name == "ln1":
                    take_root(b, 2, 1)
                elif name == "h_copy":
                    two_tiles(b, h_tiles_ready, hT_ready, hT)
                elif name.startswith("qq_copy"):
                    n = int(name[-1])
                    act.wait_ge(query_ready, 8 * b + 2 * n + 2)
                    a.activation(qqT[:, 4 * n:4 * n + 4, :].rearrange("p t q -> p (t q)"), bank[4 + n][:],
                                 ACT.Copy).then_inc(qqT_ready, 1)
                elif name.startswith("s_copy"):
                    n = int(name[-1])
                    act.wait_ge(keyscores_ready, 4 * b + n + 1)
                    a.activation(s[:, 4 * n:4 * n + 4, :].rearrange("p t q -> p (t q)"), bank[2 + n % 2][:],
                                 ACT.Copy).then_inc(s_ready, 1)
                elif name.startswith("exp"):
                    n = int(name[-1])
                    act.wait_ge(cv_shifted, 2 * b + n + 1)
                    a.activation(cv[:, 4 * n:4 * n + 4, :], cv[:, 4 * n:4 * n + 4, :], ACT.Exp).then_inc(gate_exp_ready, 1)

            def dots_of(c, g, bt):
                act.wait_ge(dots_ready, (c * GROUPS + g) * BPG + bt + 1)
                a.activation(gelu[:, bt * BATCH:(bt + 1) * BATCH], dots[:, bt * BATCH:(bt + 1) * BATCH],
                             ACT.Gelu).then_inc(gelu_ready, 1)

            def sums_of(c, g, bt, by_dve):
                if by_dve not in DIAGS_BY_ACT:
                    return
                G = c * GROUPS + g
                act.wait_ge(gather_step, G * BPG + bt + 1)
                own = summed_by_dve(bt, by_dve)
                for k in range(bt * BATCH, (bt + 1) * BATCH):
                    if k not in own:
                        act.wait_ge(slot_free[k], G + 1)
                        ins = a.activation(diags[k], ident[:], ACT.Copy, scale=wts[:, k:k + 1])
                ins.then_inc(diags_ready, 1)

            def batch(c, g, bt, by_dve):
                dots_of(c, g, bt)
                sums_of(c, g, bt, by_dve)

            def finish(c):
                act.wait_ge(var_ready, c + 1)
                a.activation(froot[:], fmv[:, 1:2], ACT.Sqrt).then_inc(froot_ready, 1)

            first_block(stages, batch)

            with act.Fori(0, LATE_GROUPS) as g:
                for j in range(2):
                    batch(0, g + EARLY_GROUPS, j, LATE_BY_DVE)
                    for tb in range(1, NB):
                        act.wait_ge(late_tiles_ready, (g * 2 + j) * LATE + tb)
                        a.activation(proj[:, ds(tb * COLS + QA + (g * 2 + j) * CW, CW)],
                                     bank[1 + 3 * j + tb][:, 0:CW], ACT.Copy).then_inc(late_tiles_copied, 1)
            in_order(stages, dots_of, sums_of, 1, (EARLY_GROUPS + LATE_GROUPS) * BPG)
            finish(0)
            with act.Fori(2, NB) as b:
                in_order(stages, dots_of, sums_of, b)
                finish(b - 1)
            with act.Fori(0, GROUPS) as g:
                for bt in range(BPG):
                    batch(NB - 1, g, bt, LAST_BY_DVE)
            finish(NB - 1)

        @block.tensor
        def _(pe):
            t_ = nc.tensor
            for k in range(RING):
                pe.sem_inc(slot_free[k], 1)
            for p in range(KV_CH):
                pe.wait_ge(wi_landed[p], 16)
                for tb in range(NB):
                    if p == 0:
                        pe.wait_ge(xT_landed[tb], 16)
                    if p >= 2:
                        pe.wait_ge(*tile_copied(p - 2, tb))
                    for k in range(KD):
                        ins = t_.matmul(bank[p % 2 * 4 + tb][:, 0:CW], xT[:, tb, k, :], wi[p][:, k, :],
                                        start=(k == 0), stop=(k == KD - 1))
                    ins.then_inc(tiles_ready, 1)

            def first_block_tile(p, in_bank, before):
                pe.wait_ge(wi_landed[p % WI_BUFS], (p // WI_BUFS + 1) * 16)
                pe.wait_ge(*before)
                for k in range(KD):
                    ins = t_.matmul(bank[in_bank][:, 0:CW], xT[:, 0, k, :], wi[p % WI_BUFS][:, k, :],
                                    start=(k == 0), stop=(k == KD - 1))
                ins.then_inc(tiles_ready, 1)

            for n in range(Q_CH):
                first_block_tile(KV_CH + n, 4 + n, tile_copied(KV_CH - 2, n))

            pe.wait_ge(keys_roped, NB)
            pe.wait_ge(*tile_copied(KV_CH + Q_CH - 1, 0))
            krot = work[:, 0:2560]
            for t in range(5):
                for kb in range(NB):
                    ins = t_.transpose(bank[2 + t][:, kb * P:(kb + 1) * P],
                                       krot[:, kb * 640 + t * P:kb * 640 + (t + 1) * P], ident[:])
                ins.then_inc(key_tiles_ready, 1)
            pe.wait_ge(kT_ready, 5)

            def landed(b, n):
                pe.wait_ge(*landed_count(b, n))

            def two_tiles(src, done):
                for n in range(2):
                    for j in range(4):
                        ins = t_.transpose(bank[2 + n][:, j * P:(j + 1) * P], src[:, (4 * n + j) * P:(4 * n + j + 1) * P],
                                           ident[:])
                    ins.then_inc(done, 1)

            def scores(b, u):
                for m in softmaxes(u):
                    if m == 0:
                        pe.wait_ge(qT_ready, 2 * b + 2)
                    if m >= 2:
                        pe.wait_ge(probs_ready, b * NSM + m - 1)
                    if u < AH:
                        g, tile, ktile = u // 4, u % 4, 0
                    else:
                        g, tile, ktile = m % 2, 4 + (u - AH), 1 + (u - AH)
                    rows = slice(g * HD, (g + 1) * HD)
                    t_.matmul(bank[2 + m % 2][:], qT[rows, tile, :], kT[rows, ktile * T:(ktile + 1) * T],
                              start=True, stop=True).then_inc(scores_ready, 1)

            def attend(b, step):
                if step == 0:
                    scores(b, 0)
                if step + 1 < UNITS:
                    scores(b, step + 1)
                u = step - 1
                if 0 <= u < UNITS:
                    if u < AH:
                        pe.wait_ge(probs_ready, b * NSM + u + 1)
                    else:
                        pe.wait_ge(combined_ready, b * BH + u - AH + 1)
                    pu = probs[softmaxes(u)[0] % 4]
                    for j in range(NB):
                        ins = t_.transpose(bank[4 + u % 2][:, j * P:(j + 1) * P], pu[:, j * P:(j + 1) * P], ident[:])
                    ins.then_inc(pT_tiles_ready, 1)
                w = step - 2
                if 0 <= w < UNITS:
                    pe.wait_ge(pT_ready, b * UNITS + w + 1)
                    free = 2 if two_o_banks(b) else 1
                    if w >= free:
                        pe.wait_ge(o_taken, b * UNITS + w + 1 - free)
                    width = HD if w < AH else 2 * HD
                    for kc in range(NB):
                        c0 = kc * COLS + (VA + (w // 4) * HD if w < AH else VB + (w - AH) * 2 * HD)
                        ins = t_.matmul(o_bank(b, w)[:, 0:width], pT[w % 2][:, kc * P:(kc + 1) * P],
                                        proj[:, c0:c0 + width], start=(kc == 0), stop=(kc == NB - 1))
                    ins.then_inc(o_ready, 1)

            def stages(name, b):
                if name == "q_tiles":
                    pe.wait_ge(q_roped, 2 * b + 2)
                    if not isinstance(b, int) or b > 0:
                        pe.wait_ge(s_ready, 4 * b)
                    two_tiles(qrot, q_tiles_ready)
                elif name.startswith("late_tile"):
                    n = int(name[9:])
                    p = LOOP_CH + n // LATE
                    pe.wait_ge(late_landed[p % 2], 16 * (p // 2 + 1))
                    pe.wait_ge(late_tiles_copied, (LOOP_CH + 2) * LATE + n)
                    for k in range(KD):
                        ins = t_.matmul(bank[7][:, 0:CW], xT_late[:, n % LATE, k, :],
                                        wbuf[:, p % 2, k * CW:(k + 1) * CW], start=(k == 0), stop=(k == KD - 1))
                    ins.then_inc(late_tiles_ready, 1)
                elif name.startswith("gate_tile"):
                    n = int(name[9:])
                    p = KV_CH + Q_CH + n
                    first_block_tile(p, n % 2, tile_copied(KV_CH - 1, n) if n < 2 else tile_copied(p - 2, 0))
                elif name.startswith("attend"):
                    attend(b, int(name[6:]))
                elif name == "y_tiles":
                    pe.wait_ge(y_ready, b + 1)
                    two_tiles(yab, y_tiles_ready)
                elif name == "branches":
                    pe.wait_ge(yT_ready, 2 * b + 2)
                    for n in range(4):
                        landed(b, BRANCH_W + n)
                        for k in range(4):
                            ins = t_.matmul(bank[4 + n][:], yT[:, 4 * (n % 2) + k, :],
                                            weights(BRANCH_W + n, k, 512),
                                            start=(k == 0), stop=(k == 3))
                        ins.then_inc(branch_ready, 1)
                elif name == "m_tiles":
                    pe.wait_ge(merged_ready, 2 * b + 2)
                    two_tiles(merged, m_tiles_ready)
                elif name == "outproj":
                    pe.wait_ge(mT_ready, 2 * b + 2)
                    for n in range(4):
                        landed(b, OUT_W + n)
                        for k in range(KD):
                            ins = t_.matmul(bank[4 + n // 2][:, n % 2 * 256:n % 2 * 256 + 256], mT[:, k, :],
                                            weights(OUT_W + n, k, 256),
                                            start=(k == 0), stop=(k == KD - 1))
                        ins.then_inc(outproj_ready, 1)
                elif name == "h_tiles":
                    pe.wait_ge(h_ready, b + 1)
                    two_tiles(h_new, h_tiles_ready)
                elif name.startswith("query"):
                    pe.wait_ge(hT_ready, 2 * b + 2)
                    for q in range(2 * int(name[-1]), 2 * int(name[-1]) + 2):
                        landed(b, QUERY_W + q)
                        for j in range(2):
                            ct = 2 * q + j
                            for k in range(KD):
                                ins = t_.matmul(bank[4 + ct // 4][:, ct % 4 * P:ct % 4 * P + P],
                                                weights(QUERY_W + q, k * 2 + j, P),
                                                hT[:, k, :], start=(k == 0), stop=(k == KD - 1))
                        ins.then_inc(query_ready, 1)
                elif name.startswith("keys"):
                    n = int(name[-1])
                    pe.wait_ge(sub_keys_landed[n % 2], 16 * (2 * b + n // 2 + 1))
                    pe.wait_ge(qqT_ready, 4 * b + n + 1)
                    if n >= 2:
                        pe.wait_ge(s_ready, 4 * b + n - 1)
                    for j in range(4):
                        ins = t_.matmul(bank[2 + n % 2][:, j * P:(j + 1) * P], qqT[:, 4 * n + j, :],
                                        sub_keys[n % 2][:, j * P:(j + 1) * P], start=True, stop=True)
                    ins.then_inc(keyscores_ready, 1)

            def clear(c):
                pe.wait_ge(y_free, c + 1)
                for n in range(2):
                    t_.matmul(bank[n][:, 0:2], zeros[:], zeros[:, 0:2], start=True, stop=False, skip_group_check=True)

            def add_slot(G, bt, k):
                pe.wait_ge(diags_ready, G * BPG + bt + 1)
                for n in range(2):
                    ins = t_.matmul(bank[n][:], diags[k], uv(k)[:, D + n * 512:D + (n + 1) * 512],
                                    start=False, stop=False, skip_group_check=True)
                ins.then_inc(slot_free[k], 1)

            def summed_by_pe(bt, by_dve):
                return [k for k in range(bt * BATCH, (bt + 1) * BATCH) if k not in summed_by_dve(bt, by_dve)]

            def dots_of(c, g, bt):
                pass

            def sums_of(c, g, bt, by_dve):
                if isinstance(g, int) and g == 0 and bt == 0:
                    clear(c)
                for k in summed_by_pe(bt, by_dve):
                    add_slot(c * GROUPS + g, bt, k)

            batch = sums_of

            pe.wait_ge(zeros_set, 1)
            first_block(stages, batch)
            pe.wait_ge(s_ready, 4)
            pe.wait_ge(xT_late_landed, 16)
            with pe.Fori(0, LATE_GROUPS) as g:
                for j in range(2):
                    pe.wait_ge(late_landed[j], g * 16 + 16)
                    w = wbuf[:, j, :].rearrange("p (k c) -> p k c", k=KD)
                    for tb in range(1, NB):
                        pe.wait_ge(late_tiles_copied, (g * 2 + j) * LATE + tb)
                        for k in range(KD):
                            ins = t_.matmul(bank[1 + 3 * j + tb][:, 0:CW], xT_late[:, tb - 1, k, :], w[:, k, :],
                                            start=(k == 0), stop=(k == KD - 1))
                        ins.then_inc(late_tiles_ready, 1)
                        for k in summed_by_pe(j, LATE_BY_DVE)[tb - 1:tb if tb < LATE else None]:
                            add_slot(g + EARLY_GROUPS, j, k)
            in_order(stages, dots_of, sums_of, 1, (EARLY_GROUPS + LATE_GROUPS) * BPG)
            with pe.Fori(2, NB) as b:
                in_order(stages, dots_of, sums_of, b)
            clear(NB - 1)
            with pe.Fori(0, GROUPS) as g:
                for bt in range(BPG):
                    batch(NB - 1, g, bt, LAST_BY_DVE)


def rope_table():
    def table(pos, dim):
        freqs = np.float32(10000.0) ** (-np.arange(0, dim, 2, dtype=np.float32) / np.float32(dim))
        ang = pos.astype(np.float32)[:, None] * freqs[None, :]
        cos, sin = np.cos(ang), np.sin(ang)
        return np.concatenate([cos, cos], 1), np.concatenate([-sin, sin], 1)

    pos = np.arange(T)
    row, col, seq = table(pos // 64, HD // 2), table(pos % 64, HD // 2), table(pos, HD)
    a = [np.concatenate([row[i], col[i]], 1) for i in range(2)]
    out = np.stack([a[0], a[1], seq[0], seq[1]]).astype(np.float32)
    return np.ascontiguousarray(out.reshape(4, NB, P, HD).transpose(2, 0, 1, 3).reshape(P, 4, NB * HD))


def kernel(**inputs):
    import concourse.bacc as bacc
    from concourse.bass_utils import run_bass_kernel_spmd

    f = {k: np.asarray(a) for k, a in inputs.items()}
    x = f["x"][0]
    w_in = f["w_in"][0]
    qa = w_in[:, 0:512].reshape(D, 2, 4, HD).transpose(0, 2, 1, 3).reshape(D, 512)
    w_in = np.concatenate([w_in[:, 512:640], w_in[:, 1280:1792], w_in[:, 640:768], w_in[:, 1792:2304], qa,
                           w_in[:, 768:1280], w_in[:, 2304:]], axis=1)
    w_in = w_in.reshape(KD, P, NCH, CW).transpose(2, 1, 0, 3).reshape(NCH * P, KD * CW)

    def pieces(w, width):
        rows, cols = w.shape
        return list(w.reshape(rows // P, P, cols // width, width).transpose(2, 1, 0, 3).reshape(-1, P, 2048))

    a, b = pieces(f["w_proj_a"][0], 512), pieces(f["w_proj_b"][0], 512)
    keys = f["sub_keys"][0].transpose(3, 0, 1, 2).reshape(P, HI * NK)
    wch = np.stack([a[0], b[0], a[1], b[1]] + pieces(f["w_out"][0], 256) + pieces(f["w_query"][0], 256) + [keys])
    arrays = {
        "x": x,
        "xT": x.reshape(NB, P, KD, P).transpose(0, 3, 2, 1).reshape(NB, P, D),
        "w_in": w_in,
        "w_chunks": wch,
        "b_gate": f["b_gate"],
        "ln1": np.concatenate([f["ln1_g"], f["ln1_b"]], axis=1),
        "ln2": np.concatenate([f["ln2_g"], f["ln2_b"]], axis=1),
        "gains": np.concatenate([f["q_norm_a"], f["k_norm_a"]], axis=1),
        "subln": f["subln_b"],
        "lambdas": np.concatenate([f["lambda_q1"], f["lambda_k1"], f["lambda_q2"], f["lambda_k2"]], axis=1),
        "rope": rope_table(),
        "ident": np.eye(P, dtype=np.float32),
        "iota": np.arange(TOPK, dtype=np.float32)[None],
        "uv": np.concatenate([f["u_table"][0], f["v_table"][0]], axis=1),
    }
    arrays = {f"in_{k}": np.ascontiguousarray(a) for k, a in arrays.items()}
    nc = bacc.Bacc("TRN2", target_bir_lowering=False, num_devices=1)
    args = [nc.dram_tensor(k, a.shape, mybir.dt.from_np(a.dtype), kind="ExternalInput").ap() for k, a in arrays.items()]
    out = nc.dram_tensor("out", (T, D), F32, kind="ExternalOutput").ap()
    build(nc, *args, out)
    r = run_bass_kernel_spmd(nc, [arrays], core_ids=[0])
    return r.results[0]["out"].reshape(1, T, D)
```
